# Optimizing a Trainium2 kernel written in Bass

```python
import math
import jax
import jax.numpy as jnp
from jax import lax
import numpy as np

D_MODEL = 2048
BATCH = 1
SEQ = 512
DEPTH = 1

CHUNK = 64
D_RNN = D_MODEL
LRU_HEADS = 8
LRU_BLOCK = D_RNN // LRU_HEADS
LRU_C = 8.0
CONV_W = 4
D_POOL = D_MODEL // 2
POOL_WINDOWS = (2, 4, 8, 16)
POOL_GROUPS = len(POOL_WINDOWS)
POOL_GW = D_POOL // POOL_GROUPS
N_BRANCH = 2
D_IN = 2 * D_RNN + D_POOL + N_BRANCH * D_MODEL
D_FF = 5632
FFN_CONV_W = 3
N_ADA = 6
EPS = 1e-6

kernel_name = "hybrid_rglru_pool_streaming_trunk"

def rms_norm(x, g):
    xf = x.astype(jnp.float32)
    y = xf * lax.rsqrt(jnp.mean(xf * xf, axis=-1, keepdims=True) + EPS)
    return (y * g.astype(jnp.float32)).astype(x.dtype)

def causal_dwconv(x, w, b):
    k_w = w.shape[0]
    s = x.shape[1]
    xp = jnp.pad(x, ((0, 0), (k_w - 1, 0), (0, 0)))
    y = b
    for k in range(k_w):
        y = y + xp[:, k:k + s] * w[k]
    return y

def _lru_combine(left, right):
    a1, b1 = left
    a2, b2 = right
    return a1 * a2, a2 * b1 + b2

def rg_lru(x, wa, ba, wx, bx, lam):
    bsz, s, _ = x.shape
    xh = x.reshape(bsz, s, LRU_HEADS, LRU_BLOCK)
    r = jax.nn.sigmoid((jnp.einsum('bshi,hij->bshj', xh, wa).reshape(bsz, s, D_RNN) + ba).astype(jnp.float32))
    i = jax.nn.sigmoid((jnp.einsum('bshi,hij->bshj', xh, wx).reshape(bsz, s, D_RNN) + bx).astype(jnp.float32))
    log_a = LRU_C * r * jax.nn.log_sigmoid(lam.astype(jnp.float32))
    a = jnp.exp(log_a)
    inp = jnp.sqrt(-jnp.expm1(2.0 * log_a)) * (i * x.astype(jnp.float32))
    _, h = lax.associative_scan(_lru_combine, (a, inp), axis=1)
    return h.astype(x.dtype)

def multiscale_pool(x, w, b, scale):
    bsz, s, _ = x.shape
    xg = x.reshape(bsz, s, POOL_GROUPS, POOL_GW).astype(jnp.float32)
    pos = jnp.arange(s, dtype=jnp.float32)
    pooled = []
    for g, win in enumerate(POOL_WINDOWS):
        xi = xg[:, :, g]
        cs0 = jnp.pad(jnp.cumsum(xi, axis=1), ((0, 0), (1, 0), (0, 0)))
        upper = cs0[:, 1:]
        lower = jnp.pad(cs0[:, :s + 1 - win], ((0, 0), (win - 1, 0), (0, 0)))
        count = jnp.minimum(pos + 1.0, float(win))[None, :, None]
        pooled.append((upper - lower) / count - xi)
    p = jnp.stack(pooled, axis=2).astype(x.dtype)
    y = jnp.einsum('bsgc,gcd->bsgd', p, w).reshape(bsz, s, D_POOL) + b
    return y * scale

def setup_inputs(seed: int = 0) -> dict:
    key = jax.random.key(seed)
    ks = jax.random.split(key, 32)
    L, D = DEPTH, D_MODEL
    f32 = jnp.float32

    def nrm(k, shape, fan_in, mult=1.0):
        return jax.random.normal(k, shape, f32) * (mult * fan_in ** -0.5)

    def small(k, shape, s=0.02):
        return jax.random.normal(k, shape, f32) * s

    u = jax.random.uniform(ks[10], (L, D_RNN), f32, 0.9, 0.999)
    sig = u ** (1.0 / LRU_C)
    lam = jnp.log(sig) - jnp.log1p(-sig)

    return {
        "x": jax.random.normal(ks[0], (BATCH, SEQ, D), f32),
        "c": jax.random.normal(ks[1], (BATCH, D), f32),
        "ada_w": nrm(ks[2], (L, D, N_ADA * D), D, 0.5),
        "ada_b": small(ks[3], (L, N_ADA * D)),
        "norm_mix_g": 1.0 + small(ks[4], (L, D)),
        "w_in": nrm(ks[5], (L, D, D_IN), D),
        "b_in": small(ks[6], (L, D_IN)),
        "conv_w": nrm(ks[7], (L, CONV_W, D_RNN), CONV_W),
        "conv_b": small(ks[8], (L, D_RNN)),
        "lru_wa": nrm(ks[9], (L, LRU_HEADS, LRU_BLOCK, LRU_BLOCK), LRU_BLOCK),
        "lru_ba": small(ks[11], (L, D_RNN)),
        "lru_wx": nrm(ks[12], (L, LRU_HEADS, LRU_BLOCK, LRU_BLOCK), LRU_BLOCK),
        "lru_bx": small(ks[13], (L, D_RNN)),
        "lru_lambda": lam,
        "pool_w": nrm(ks[14], (L, POOL_GROUPS, POOL_GW, POOL_GW), POOL_GW),
        "pool_b": small(ks[15], (L, D_POOL)),
        "pool_scale": 1.0 + small(ks[16], (L, D_POOL), 0.1),
        "proj_a": nrm(ks[17], (L, D_RNN, D), D_RNN),
        "proj_b": nrm(ks[18], (L, D_POOL, D), D_POOL),
        "w_out": nrm(ks[19], (L, D, D), D),
        "norm_ffn_g": 1.0 + small(ks[20], (L, D)),
        "w_up": nrm(ks[21], (L, D, 2 * D_FF), D),
        "ffn_conv_w": nrm(ks[22], (L, FFN_CONV_W, 2 * D_FF), FFN_CONV_W),
        "ffn_conv_b": small(ks[23], (L, 2 * D_FF)),
        "w_down": nrm(ks[24], (L, D_FF, D), D_FF),
        "final_g": 1.0 + small(ks[25], (D,)),
    }

def reference(x, c, ada_w, ada_b, norm_mix_g, w_in, b_in, conv_w, conv_b,
              lru_wa, lru_ba, lru_wx, lru_bx, lru_lambda, pool_w, pool_b,
              pool_scale, proj_a, proj_b, w_out, norm_ffn_g, w_up, ffn_conv_w,
              ffn_conv_b, w_down, final_g):
    c_act = jax.nn.silu(c)
    for l in range(DEPTH):
        mod = c_act @ ada_w[l] + ada_b[l]
        sh1, sc1, gt1, sh2, sc2, gt2 = [m[:, None, :] for m in jnp.split(mod, N_ADA, axis=-1)]

        h = rms_norm(x, norm_mix_g[l]) * (1.0 + sc1) + sh1
        z = h @ w_in[l] + b_in[l]
        x_rnn, g_rnn, x_pool, g_br = jnp.split(
            z, [D_RNN, 2 * D_RNN, 2 * D_RNN + D_POOL], axis=-1)
        xr = causal_dwconv(x_rnn, conv_w[l], conv_b[l])
        ya = rg_lru(xr, lru_wa[l], lru_ba[l], lru_wx[l], lru_bx[l], lru_lambda[l])
        ya = ya * jax.nn.gelu(g_rnn)
        yb = multiscale_pool(x_pool, pool_w[l], pool_b[l], pool_scale[l])
        gate_a, gate_b = jnp.split(jax.nn.sigmoid(g_br), N_BRANCH, axis=-1)
        merged = gate_a * (ya @ proj_a[l]) + gate_b * (yb @ proj_b[l])
        x = x + gt1 * (merged @ w_out[l])

        h = rms_norm(x, norm_ffn_g[l]) * (1.0 + sc2) + sh2
        up = causal_dwconv(h @ w_up[l], ffn_conv_w[l], ffn_conv_b[l])
        u_act, u_lin = jnp.split(up, 2, axis=-1)
        x = x + gt2 * ((jax.nn.silu(u_act) * u_lin) @ w_down[l])

    return rms_norm(x, final_g)


_drawn_inputs = setup_inputs


def setup_inputs(seed=0):
    import zlib

    import numpy as np

    out = dict(_drawn_inputs(seed))
    spreads = {}
    factors = {'norm_mix_g': 8.0,
     'b_in': 4.934,
     'conv_b': 4.944,
     'lru_wa': 2.674,
     'lru_ba': 45.294,
     'lru_bx': 21.689,
     'pool_b': 22.136,
     'pool_scale': 3.803,
     'norm_ffn_g': 8.0,
     'ffn_conv_b': 8.0,
     'final_g': 2.718}
    for name, (base, spread) in spreads.items():
        noise = np.random.default_rng([zlib.crc32(name.encode()), seed]).standard_normal(out[name].shape)
        drawn = base * np.exp(spread * noise) if base else spread * noise
        out[name] = jnp.asarray(drawn.astype(out[name].dtype))
    for name, factor in factors.items():
        out[name] = (out[name] * factor).astype(out[name].dtype)
    return out
```

```python
import concourse.bass as bass
from concourse import mybir
from contextlib import ExitStack

F32 = mybir.dt.float32
F32R = mybir.dt.float32r
ALU = mybir.AluOpType
ACT = mybir.ActivationFunctionType

P = 128
KB = 1024
QT = 4
UC = 256
EPS = 1e-6
LRU_C = 8.0
WINDOWS = (2, 4, 8, 16)
PAD = 16
RAW, SPLIT = 4, 2
STAGE0 = 7
CHUNK = 2
STAGE = 4
MC = 512


class Steps:

    def __init__(self, sem):
        self.sem, self.n, self.i, self.per = sem, 0, None, 0

    def done(self, instruction):
        self.n += 1
        instruction.then_inc(self.sem, 1)

    def wait(self, engine):
        engine.wait_ge(self.sem, self.n if self.i is None else self.i * self.per + self.n)

    def loop(self, i, per):
        self.i, self.per, self.first = i, per, self.n

    def end(self, turns):
        assert self.n - self.first == self.per, (self.n - self.first, self.per)
        self.n = self.first + self.per * turns
        self.i = None


def trunk_kernel(nc, x, c, ada_w, ada_b, norm_mix_g, w_in, b_in, conv_w, conv_b, lru_wa, lru_ba, lru_wx,
                 lru_bx, lru_lambda, pool_w, pool_b, pool_scale, proj_a, proj_b, w_out, norm_ffn_g, w_up,
                 ffn_conv_w, ffn_conv_b, w_down, final_g, out):
    S, D = x.shape[1], x.shape[2]
    NT = D // P
    ST = S // P
    NQ = NT // QT
    DF = w_down.shape[1]
    GROUPS = DF // P // QT
    HEADS = lru_wa.shape[1]
    TAPS = conv_w.shape[1]
    PAIRS = NT // 2
    PT = pool_b.shape[1] // P
    GT, XP, GA, GB = NT, 2 * NT, 2 * NT + PT, 3 * NT + PT
    assert (S, NT, NQ, HEADS, PAIRS, PT, TAPS) == (512, 16, 4, 8, 8, 8, 4) and lru_wa.shape[2] == UC

    U_P3 = NQ * 3
    U_GB0 = U_P3 + NQ
    U_PW = U_GB0 + NQ
    U_GB1 = U_PW + 2
    U_B = U_GB1 + NQ
    B_SEG = 6
    B_TURNS = 3
    EARLY = 2
    R_BLOCK = EARLY + 2 * B_TURNS
    U_B2 = U_B + 2 * B_SEG * B_TURNS
    U_R = U_B2 + 4
    R_SEG = 9
    R_HEADS = 4
    R_TURNS = HEADS // R_HEADS
    U_M = U_R + R_SEG * HEADS
    U_O = U_M + 8 * PAIRS
    U_F = U_O + 4 * PAIRS
    U_L = U_F + 16
    F_SEG = 24
    U_D = U_L + F_SEG * (GROUPS - 1)
    UNITS = U_D + 8
    TWO = R_TURNS

    def rows(w):
        return w.rearrange("(t p) n -> p t n", p=P)

    win_v, wup_v, wdn_v, wout_v = rows(w_in[0]), rows(w_up[0]), rows(w_down[0]), rows(w_out[0])
    pa_v, pb_v, ada_v = rows(proj_a[0]), rows(proj_b[0]), rows(ada_w[0])
    pw_v = pool_w[0].rearrange("g (k p) n -> p (g k) n", p=P)
    wa_v = lru_wa[0].rearrange("h (k p) n -> p (h k) n", p=P)
    wx_v = lru_wx[0].rearrange("h (k p) n -> p (h k) n", p=P)
    x_v = x[0].rearrange("(s p) d -> p s d", p=P)
    out_v = out[0].rearrange("(s p) d -> p s d", p=P)
    resid_spill = nc.dram_tensor("resid_spill", (P, NT, S), F32, kind="Internal").ap()
    pool_spill = nc.dram_tensor("pool_spill", (P, NT, S), F32, kind="Internal").ap()

    def by_tile(v):
        return v.rearrange("a (t p) -> (a t) p", p=P)

    FT = 2 * DF // P
    packs = [[("c", c), ("g_mix", norm_mix_g), ("ada_b", ada_b)],
             [("b_in", b_in), ("conv_b", conv_b), ("ba", lru_ba), ("bx", lru_bx), ("pool_b", pool_b)],
             [("conv_w", conv_w[0]), ("lam", lru_lambda), ("pool_s", pool_scale), ("g_ffn", norm_ffn_g),
              ("g_out", final_g.rearrange("(a n) -> a n", a=1))],
             [("ffn_b", ffn_conv_b)],
             [("ffn_w0", ffn_conv_w[0][0:1])], [("ffn_w1", ffn_conv_w[0][1:2])], [("ffn_w2", ffn_conv_w[0][2:3])]]
    NP = len(packs)
    place, pack_rows, param_loads = {}, [], []
    for n, pack in enumerate(packs):
        at = 0
        for name, v in pack:
            count = v.shape[0] * v.shape[1] // P
            place[name] = n * P + at
            param_loads.append((n, at, count, by_tile(v)))
            at += count
        assert at <= P
        pack_rows.append(at)

    ctx = ExitStack()
    with ctx:
        def sem(name):
            return ctx.enter_context(nc.semaphore(name))

        base = -(-nc.sbuf_base // 64) * 64
        top = [0]

        def at(name, shape, dt, offset):
            size = 4
            for n in shape[1:]:
                size *= n
            top[0] = max(top[0], offset + size)
            return nc.alloc_sbuf_tensor_at(name, shape, dt, offset=base + offset)

        TILE = 4 * S
        PAIR = 2 * TILE
        A, B, B2, C = 0, 64 * KB, 96 * KB, 128 * KB
        col_hi = at("col_hi", [P, NT, S], F32R, A)
        col_lo = at("col_lo", [P, NT, S], F32R, A + 32 * KB)
        pack_in = at("pack_in", [P, NP, P], F32, A)
        square_out = at("square_out", [P, D], F32, A + 8 * KB)
        rows_out = at("rows_out", [P, ST, D], F32, A)
        br_hi = at("br_hi", [P, NT, S], F32R, B)
        br_lo = at("br_lo", [P, NT, S], F32R, B + 32 * KB)
        x_rows = at("x_rows", [P, ST, D], F32, B)
        xn = at("xn", [P, NT, S], F32, B)
        ada_stage0 = at("ada_stage0", [P, STAGE0, CHUNK, MC], F32, B2)
        ada_acc0 = at("ada_acc0", [P, 2, MC], F32, B2 + STAGE0 * 4 * KB)
        yb_hi = at("yb_hi", [P, PT, S], F32R, B)
        yb_lo = at("yb_lo", [P, PT, S], F32R, B + 16 * KB)
        pool_hi = at("pool_hi", [P, PT, S], F32R, B2)
        pool_lo = at("pool_lo", [P, PT, S], F32R, B2 + 16 * KB)
        resid = at("resid", [P, NT, S], F32, B)
        u_hi = at("u_hi", [P, QT, S], F32R, B2)
        u_lo = at("u_lo", [P, QT, S], F32R, B2 + 8 * KB)
        sq = at("sq", [P, 2, S], F32, B2 + 16 * KB)
        sq_sum = at("sq_sum", [P, S], F32, B2 + 20 * KB)
        h2f = at("h2f", [P, QT, S], F32, B2 + 22 * KB)
        xT = at("xT", [P, NT, S], F32, C)
        z = at("z", [P, 2, PAD + S], F32, C)
        Z1 = C + 8 * (PAD + S)
        win_a = at("win_a", [P, 2, PAD + S], F32, Z1)
        win_b = at("win_b", [P, 2, PAD + S], F32, Z1 + 8 * (PAD + S))
        Z2 = Z1 + 16 * (PAD + S)
        ybf = at("ybf", [P, 2, S], F32, Z2)
        gate_b = at("gate_b", [P, 2, 2, S], F32, Z2 + PAIR)
        pbf = at("pbf", [P, 2, S], F32, Z2 + 3 * PAIR)
        count_fix = at("count_fix", [P, len(WINDOWS), 2, PAD], F32, Z2 + 4 * PAIR)
        xr = at("xr", [P, 2, S], F32, Z1)
        xr_hi = at("xr_hi", [P, 2, S], F32R, Z1 + PAIR)
        xr_lo = at("xr_lo", [P, 2, S], F32R, Z1 + 2 * PAIR)
        decay = at("decay", [P, 2, S], F32, Z1 + 3 * PAIR)
        inp = at("inp", [P, 2, S], F32, Z1 + 4 * PAIR)
        tanh_q = at("tanh_q", [P, 2, S], F32, Z1 + 5 * PAIR)
        gelu = at("gelu", [P, 2, S], F32, Z1 + 6 * PAIR)
        merged = at("merged", [P, NT, S], F32, C)
        conv_a = at("conv_a", [P, 2, S], F32, C)
        conv_l = at("conv_l", [P, 2, S], F32, C + PAIR)
        silu_a = at("silu_a", [P, 2, 2, S], F32, C + 2 * PAIR)
        scaled = at("scaled", [P, 2, 2, S], F32, C + 4 * PAIR)
        W = Z1 + 7 * PAIR
        UNIT = 4 * QT * UC
        w_raw = at("w_raw", [P, RAW, QT, UC], F32, W)
        w_hi = at("w_hi", [P, SPLIT, QT, UC], F32R, W + RAW * UNIT)
        w_lo = at("w_lo", [P, SPLIT, QT, UC], F32R, W + (RAW + SPLIT) * UNIT)
        K = W + (RAW + 2 * SPLIT) * UNIT
        par = at("par", [P, NP * P], F32, K)
        mod = at("mod", [P, 6 * NT], F32, K + 4 * NP * P)
        K2 = K + 4 * NP * P + 24 * NT
        ident = at("ident", [P, P], F32, K2)
        ones = at("ones", [P, P], F32, K2 + 512)
        K3 = K2 + 1024
        names = ["cact", "gain1", "gain2", "lam_abs", "lam_neg", "sig_l", "ser_s", "ser_s2", "ser_p", "rate", "neg_rate"]
        small = {n: at(n, [P, NT], F32, K3 + 4 * NT * k) for k, n in enumerate(names)}
        row_sq = at("row_sq", [P, ST], F32, K3 + 4 * NT * len(names))
        row_rstd = at("row_rstd", [P, ST], F32, K3 + 4 * NT * len(names) + 32)
        K4 = K3 + 4 * NT * len(names) + 64
        ada_acc = at("ada_acc", [P, MC], F32, K4)
        rstd_bc = at("rstd_bc", [P, S], F32, K4)
        ada_stage = at("ada_stage", [P, STAGE, MC], F32, K4 + 4 * MC)
        rstd_wide = at("rstd_wide", [P, ST, P], F32, K4 + 4 * MC)
        gate_a = at("gate_a", [P, 2, S], F32, K4 + 4 * MC)
        pb_in = at("pb_in", [P, 2, S], F32, K4 + 4 * MC + PAIR)
        assert base + top[0] <= nc.sbuf_usable_end, (base + top[0], nc.sbuf_usable_end)

        ps = ctx.enter_context(nc.psum_tensor("ps", [P, 8, S], F32))

        def col(name, t, n=1):
            if isinstance(t, int):
                return par[:, place[name] + t:place[name] + t + n]
            return par[:, bass.ds(t + place[name], n)]

        def cols(tensor, t, n=1):
            return tensor[:, t:t + n] if isinstance(t, int) else tensor[:, bass.ds(t, n)]

        SH1, SC1, GT1, SH2, SC2, GT2 = (k * NT for k in range(6))

        w_loaded = [sem(f"w_loaded{k}") for k in range(RAW)]
        hi_made, lo_made, unit_done = sem("hi_made"), sem("lo_made"), sem("unit_done")
        params_in, x_in = sem("params_in"), [sem(f"x_in{s}") for s in range(ST)]
        ada0_in = [sem(f"ada0_in{k}") for k in range(STAGE0)]
        ada_in = [sem(f"ada_in{k}") for k in range(STAGE)]
        const_ready, pads_ready = sem("const_ready"), sem("pads_ready")
        par_turned, par_ready, sig_c, cact_ready = sem("par_turned"), sem("par_ready"), sem("sig_c"), sem("cact_ready")
        sq_rows, rstd_rows, rstd_cast, rstd_ready = sem("sq_rows"), sem("rstd_rows"), sem("rstd_cast"), sem("rstd_ready")
        std_rows, rstd_spread = sem("std_rows"), sem("rstd_spread")
        x_turned, xT_ready, xn_ready = sem("x_turned"), sem("xT_ready"), sem("xn_ready")
        mac0, reduced0, mod0_ready, gain1_ready = sem("mac0"), sem("reduced0"), sem("mod0_ready"), sem("gain1_ready")
        h_ready, h_hi, h_lo = sem("h_ready"), sem("h_hi"), sem("h_lo")
        spilled = sem("spilled")
        z_ready, pool_f, pool_hi_ready, pool_lo_ready = sem("z_ready"), sem("pool_f"), sem("pool_hi_ready"), sem("pool_lo_ready")
        yb_f, yb_hi_ready, yb_lo_ready = sem("yb_f"), sem("yb_hi_ready"), sem("yb_lo_ready")
        gate_ready, pb_made = sem("gate_ready"), sem("pb_made")
        mac, reduced, mod_ready = sem("mac"), sem("reduced"), sem("mod_ready")
        rate_in, lam_sig, rate_ready = sem("rate_in"), sem("lam_sig"), sem("rate_ready")
        r_ready, tanh_ready = sem("r_ready"), sem("tanh_ready")
        xr_ready, xr_hi_ready, xr_lo_ready = sem("xr_ready"), sem("xr_hi_ready"), sem("xr_lo_ready")
        gates_ready, decay_ready, decay_sq = sem("gates_ready"), sem("decay_ready"), sem("decay_sq")
        var_ready, root_ready, gelu_ready = sem("var_ready"), sem("root_ready"), sem("gelu_ready")
        ya_f, ya_hi_ready, ya_lo_ready = sem("ya_f"), sem("ya_hi_ready"), sem("ya_lo_ready")
        pb_back, merged_ready, mg_hi, mg_lo = sem("pb_back"), sem("merged_ready"), sem("mg_hi"), sem("mg_lo")
        resid_in = [sem(f"resid_in{q}") for q in range(NQ)]
        x2_ready, sq_ready, sq_used = sem("x2_ready"), sem("sq_ready"), sem("sq_used")
        sum2, var2, std2, xn2_ready, h2_ready = sem("sum2"), sem("var2"), sem("std2"), sem("xn2_ready"), sem("h2_ready")
        h2_hi, h2_lo = sem("h2_hi"), sem("h2_lo")
        tap_ready, conv_ready, silu_ready = sem("tap_ready"), sem("conv_ready"), sem("silu_ready")
        uf_ready, u_hi_ready, u_lo_ready, down_added = sem("uf_ready"), sem("u_hi_ready"), sem("u_lo_ready"), sem("down_added")
        scaled_ready, turned, rows_ready = sem("scaled_ready"), sem("turned"), sem("rows_ready")
        sum3, var3, std3, rstd3 = sem("sum3"), sem("var3"), sem("std3"), sem("rstd3")
        rows_act, rows_dve, out_stored = sem("rows_act"), sem("rows_dve"), sem("out_stored")
        steps_v = sem("steps_v")

        first_blocks = [b for q in range(NQ) for b in (SC1 // QT + q, SH1 // QT + q)]
        LATER = GT1 // QT
        CH = NT // CHUNK
        QC = 2 * CH
        SPLIT_FIRST = 13
        H_LO_AFTER = 4
        SPLIT_AFTER = (9, 13, 17)
        split_due = {QC * (q + 1) + k: 3 * q + 2 + r for q in range(NQ - 1) for r, k in enumerate(SPLIT_AFTER)}
        h_lo_due = {QC * (q + 1) + H_LO_AFTER: q for q in range(NQ - 1)}
        B_FEED = (0, 1, 2, 3)
        R_FEED = (0, 1, 2, 4)
        R_SUM = (1, 2, 4, 5)

        EARLY_FEED = ((U_P3, U_P3 + 1, U_P3 + 3, U_GB0), (U_GB0 + 2, U_PW + 1, U_GB1, U_GB1 + 1))
        EARLY_SUM = ((U_P3 + 1, U_P3 + 2, U_GB0, U_GB0 + 1), (U_GB0 + 3, U_GB1, U_GB1 + 1, U_GB1 + 2))
        LRU_UNITS = [U_R + R_SEG * k + 6 for k in range(R_HEADS)]
        assert sorted(u % RAW for u in LRU_UNITS) == list(range(RAW))

        def lru_extra(u):
            return sum(k % RAW == u % RAW and k <= u for k in LRU_UNITS), 1

        def win_of(p):
            return (win_a, win_b)[p % 2]

        def span(start, n):
            return slice(start, start + n) if isinstance(start, int) else bass.ds(start, n)

        block = ctx.enter_context(nc.Block())

        @block.sync
        def _(sp):
            def load(u, src, i=None, n=0, dst=None):
                if i is not None:
                    sp.wait_ge(lo_made, i * n + (u - RAW + 1))
                elif u >= RAW:
                    sp.wait_ge(lo_made, u - RAW + 1)
                sp.dma_start(w_raw[:, u % RAW] if dst is None else dst, src).then_inc(w_loaded[u % RAW], 16)

            def at_reg(v):
                return v if isinstance(v, int) else sp.snap(v)

            def win(tile, q):
                return win_v[:, q * QT:(q + 1) * QT, span(at_reg(tile * P), UC)]

            def ada0(n):
                blk, k = first_blocks[n // CH], n % CH
                if n >= STAGE0:
                    sp.wait_ge(mac0, CHUNK * (n - STAGE0 + 1))
                sp.dma_start(ada_stage0[:, n % STAGE0], ada_v[:, k * CHUNK:(k + 1) * CHUNK, blk * MC:(blk + 1) * MC]
                             ).then_inc(ada0_in[n % STAGE0], 16)

            def p_unit(u):
                return win(XP + 2 * (u % 3), u // 3) if u < U_P3 else win(XP + 6, u - U_P3)

            for n, a, count, v in param_loads:
                sp.dma_start(pack_in[a:a + count, n], v).then_inc(params_in, 16)
            for n in range(STAGE0):
                ada0(n)
            for s in range(ST):
                sp.dma_start(x_rows[:, s], x_v[:, s]).then_inc(x_in[s], 16)
            for u in range(RAW):
                load(u, p_unit(u))
            for n in range(STAGE0, QC * NQ):
                ada0(n)
                if n - STAGE0 in (SPLIT_FIRST + 1, SPLIT_FIRST + 2):
                    u = n - STAGE0 - SPLIT_FIRST - 1 + RAW
                    load(u, p_unit(u))
                if n - STAGE0 in split_due:
                    u = split_due[n - STAGE0] + RAW
                    load(u, p_unit(u))
            sp.wait_ge(xT_ready, NT)
            sp.dma_start(resid_spill, xT[:]).then_inc(spilled, 16)
            for u in range(max(v for c_, v in split_due.items() if c_ + STAGE0 < QC * NQ) + 1 + RAW, U_GB0):
                load(u, p_unit(u))
            for q in range(NQ):
                load(U_GB0 + q, win(GB, q))
            for k in range(2):
                load(U_PW + k, pw_v[:, k * QT:(k + 1) * QT, :])
            for q in range(NQ):
                load(U_GB1 + q, win(GB + 2, q))

            def proj_b_unit(j, k):
                return pb_v[:, k * QT:(k + 1) * QT, span(at_reg(j * UC), UC)]

            with sp.Fori(0, B_TURNS) as i:
                for half in range(2):
                    for k in range(B_SEG):
                        j = i * 2 + half
                        load(U_B + half * B_SEG + k, proj_b_unit(j, k) if k < 2 else win(j * 2 + (GB + 4), k - 2),
                             i, 2 * B_SEG)
            for k in range(4):
                load(U_B2 + k, proj_b_unit(2 * B_TURNS + k // 2, k % 2))

            with sp.Fori(0, R_TURNS) as i:
                for head in range(R_HEADS):
                    for k in range(R_SEG):
                        u, n = U_R + head * R_SEG + k, R_SEG * R_HEADS
                        tile = i * (2 * R_HEADS) + 2 * head
                        if k == 6:
                            rows_of = bass.ds(sp.snap(tile), 2)
                            load(u, wa_v[:, rows_of, :], i, n, w_raw[:, u % RAW, 0:2])
                            sp.dma_start(w_raw[:, u % RAW, 2:4], wx_v[:, rows_of, :]).then_inc(w_loaded[u % RAW], 16)
                        else:
                            load(u, win(tile, k) if k < 4 else win(tile + GT, k - 4 if k < 6 else k - 5), i, n)

            with sp.Fori(0, PAIRS) as i:
                for k in range(8):
                    load(U_M + k, win(i * 2 + GA, k) if k < 4 else
                         pa_v[:, (k - 4) * QT:(k - 3) * QT, bass.ds(sp.snap(i * UC), UC)], i, 8)

            def out_unit(k, d):
                return wout_v[:, k * QT:(k + 1) * QT, span(at_reg(d * UC), UC)]

            for k in range(4):
                load(U_O + k, out_unit(k, 0))
            sp.wait_ge(unit_done, U_O)
            sp.wait_ge(spilled, 16 * (PAIRS + 1))
            for k in range(4):
                cs = slice(k * QT, (k + 1) * QT)
                sp.dma_start(resid[:, cs], resid_spill[:, cs]).then_inc(resid_in[k], 16)
                load(U_O + 4 + k, out_unit(k, 1))
            with sp.Fori(0, 3) as i:
                for half in range(2):
                    for k in range(4):
                        load(U_O + 8 + half * 4 + k, out_unit(k, i * 2 + (half + 2)), i, 8)

            def up(q, g, p):
                return wup_v[:, q * QT:(q + 1) * QT, span(at_reg(g * (QT * P) + ((p // 2) * UC + (p % 2) * DF)), UC)]

            def down(d, g):
                return wdn_v[:, span(at_reg(g * QT), QT), d * UC:(d + 1) * UC]

            for q in range(NQ):
                for p in range(4):
                    load(U_F + 4 * q + p, up(q, 0, p))
            with sp.Fori(0, GROUPS - 1) as i:
                for k in range(F_SEG):
                    load(U_L + k, up(k, i + 1, 0) if k < 4 else down(k - 4, i) if k < 12 else
                         up(k % 4, i + 1, (k - 8) // 4), i, F_SEG)
            for d in range(8):
                load(U_D + d, down(d, GROUPS - 1))
            for s in range(ST):
                sp.wait_ge(rows_act if s % 2 else rows_dve, s // 2 + 1)
                sp.dma_start(out_v[:, s], rows_out[:, s]).then_inc(out_stored, 16)
            sp.wait_ge(out_stored, 16 * ST)

        @block.gpsimd
        def _(pool):
            pool.memset(ones[:], 1.0).then_inc(const_ready, 1)
            pool.memset(ident[:], 0.0).then_inc(const_ready, 1)
            pool.wait_ge(const_ready, 2)
            pool.affine_select(out=ident[:], in_=ident[:], compare_op=ALU.not_equal, fill=1.0, base=0,
                               pattern=[[-1, P]], channel_multiplier=1).then_inc(const_ready, 1)
            pool.wait_ge(xT_ready, NT)
            pool.wait_ge(rstd_ready, 1)
            for t in range(NT):
                pool.tensor_tensor(xn[:, t], xT[:, t], rstd_bc[:], ALU.mult).then_inc(xn_ready, 1)
            pool.wait_ge(spilled, 16)
            pool.wait_ge(xn_ready, NT)
            pool.memset(z[:, :, 0:PAD], 0.0)
            pool.memset(count_fix[:], 1.0).then_inc(pads_ready, 1)
            pool.wait_ge(pads_ready, 1)
            for g, win_ in enumerate(WINDOWS):
                for t in range(win_ - 1):
                    last = pool.memset(count_fix[:, g, :, t:t + 1], win_ / (t + 1.0))
            last.then_inc(pads_ready, 1)

        @block.tensor
        def _(pe):
            def products(u, outs, hi, lo, ks=range(QT), start=True, stop=True, slot_of=None, last=True, i=None, n=0,
                         wait=True, tile_ready=None):
                if wait:
                    pe.wait_ge(lo_made, u + 1 if i is None else i * n + (u + 1))
                s = u % SPLIT
                order = [(m, a) for m in range(len(outs)) for a in range(len(ks))]
                if tile_ready is not None:
                    order.sort(key=lambda ma: ma[1])
                for m, a in order:
                        o, k = outs[m], ks[a]
                        if tile_ready is not None and m == 0:
                            pe.wait_ge(tile_ready, k + 1)
                        block_of = k if slot_of is None else slot_of[a]
                        wh = w_hi[:, s, block_of, m * P:(m + 1) * P]
                        wl = w_lo[:, s, block_of, m * P:(m + 1) * P]
                        pe.matmul(o, wh, hi(k), start=start and a == 0, stop=False)
                        pe.matmul(o, wh, lo(k), start=False, stop=False)
                        mm = pe.matmul(o, wl, hi(k), start=False, stop=stop and a == len(ks) - 1)
                if last:
                    mm.then_inc(unit_done, 1)

            def banks(b):
                return [ps[:, b], ps[:, b + 1]]

            def tiles(hi, lo, q):
                return (lambda k: hi[:, q * QT + k]), (lambda k: lo[:, q * QT + k])

            def over_model(u, b, hi, lo, i=None, n=0, nq=NQ, qs=None):
                for q in range(nq) if qs is None else qs:
                    products(u + q, banks(b), *tiles(hi, lo, q), start=q == 0, stop=q == nq - 1, i=i, n=n)

            pe.wait_ge(const_ready, 3)
            pe.wait_ge(params_in, 16 * len(param_loads))
            for n in range(NP):
                r = pack_rows[n]
                mm = pe.transpose(ps[:, 6 + n // 4, (n % 4) * P:(n % 4) * P + r], pack_in[0:r, n], ident[0:r, 0:r])
            mm.then_inc(par_turned, 1)
            for s in range(ST):
                pe.wait_ge(x_in[s], 16)
            for t in range(NT):
                if t >= 4:
                    pe.wait_ge(xT_ready, t - 3)
                for s in range(ST):
                    mm = pe.transpose(ps[:, t % 4, s * P:(s + 1) * P], x_rows[:, s, t * P:(t + 1) * P], ident[:])
                mm.then_inc(x_turned, 1)

            def spread(bank):
                for s in range(ST):
                    mm = pe.matmul(ps[:, bank, s * P:(s + 1) * P], rstd_wide[:, s], ident[:], start=True, stop=True)
                mm.then_inc(rstd_spread, 1)

            def position_sums(pairs, bank, sem_):
                pe.wait_ge(sq_used, pairs)
                for s in range(ST):
                    mm = pe.matmul(ps[:, bank, s:s + 1], sq_sum[:, s * P:(s + 1) * P], ones[:, 0:1], start=True, stop=True)
                mm.then_inc(sem_, 1)

            def reduce0(b):
                pe.wait_ge(mac0, NT * (b + 1))
                for m in range(QT):
                    mm = pe.matmul(ps[:, 7, b * QT + m:b * QT + m + 1], ada_acc0[:, b % 2, m * P:(m + 1) * P],
                                   ones[:, 0:1], start=True, stop=True)
                mm.then_inc(reduced0, 1)

            def reduce(seg, bank, i=None, segs=0):
                pe.wait_ge(mac, NT * (seg + 1) if i is None else i * (segs * NT) + NT * (seg + 1))
                for m in range(QT):
                    mm = pe.matmul(ps[:, bank, m:m + 1], ada_acc[:, m * P:(m + 1) * P], ones[:, 0:1], start=True, stop=True)
                mm.then_inc(reduced, 1)

            pe.wait_ge(rstd_cast, 1)
            pe.wait_ge(par_ready, 1)
            spread(6)
            reduce0(0)
            reduce0(1)
            for q in range(NQ):
                pe.wait_ge(h_lo, q + 1)
                for p in range(3):
                    products(3 * q + p, banks(2 * p), *tiles(col_hi, col_lo, q), start=q == 0, stop=q == NQ - 1)
                    if q < NQ - 1 and p != 1:
                        reduce0(2 * q + 2 + p // 2)
            pe.wait_ge(mod0_ready, 2 * NQ)
            over_model(U_P3, 6, col_hi, col_lo)
            over_model(U_GB0, 0, col_hi, col_lo, qs=(0, 1, 2))
            pe.wait_ge(z_ready, len(WINDOWS))
            reduce(0, 7)
            over_model(U_GB0, 0, col_hi, col_lo, qs=(3,))
            pe.wait_ge(pool_lo_ready, len(WINDOWS))
            for g, b in enumerate((2, 4, 6, 0)):
                if g == 3:
                    pe.wait_ge(gate_ready, 1)
                products(U_PW + g // 2, banks(b), (lambda k, g=g: pool_hi[:, 2 * g + k]),
                         (lambda k, g=g: pool_lo[:, 2 * g + k]), ks=range(2), slot_of=[2 * (g % 2), 2 * (g % 2) + 1],
                         last=g % 2 == 1, wait=g % 2 == 0)
            pe.wait_ge(yb_f, 1)
            over_model(U_GB1, 2, col_hi, col_lo)
            pe.wait_ge(yb_f, 3)
            with pe.Fori(0, B_TURNS) as i:
                for half in range(2):
                    u = U_B + half * B_SEG
                    over_model(u, 4, yb_hi, yb_lo, i, 2 * B_SEG, nq=2, qs=(0,))
                    reduce(EARLY + half - 1, 7, i, 2)
                    over_model(u, 4, yb_hi, yb_lo, i, 2 * B_SEG, nq=2, qs=(1,))
                    over_model(u + 2, 0, col_hi, col_lo, i, 2 * B_SEG)
            for j in range(2):
                over_model(U_B2 + 2 * j, (4, 2)[j], yb_hi, yb_lo, nq=2)
            with pe.Fori(0, R_TURNS) as i:
                n = R_SEG * R_HEADS
                for head in range(R_HEADS):
                    u, seg = U_R + head * R_SEG, R_BLOCK + head
                    over_model(u, 0, col_hi, col_lo, i, n, qs=(0,))
                    reduce(seg - 1, 4, i, R_HEADS)
                    over_model(u, 0, col_hi, col_lo, i, n, qs=(1, 2, 3))
                    over_model(u + 4, 2, col_hi, col_lo, i, n, qs=(0, 1))
                    pe.wait_ge(xr_lo_ready, i * R_HEADS + (head + 1))
                    for gate in range(2):
                        products(u + 6, banks(4 + 2 * gate), lambda k: xr_hi[:, k], lambda k: xr_lo[:, k], ks=range(2),
                                 slot_of=[2 * gate, 2 * gate + 1], last=gate == 1, wait=gate == 0, i=i, n=n)
                    over_model(u + 5, 2, col_hi, col_lo, i, n, qs=(2, 3))
            pe.wait_ge(gates_ready, HEADS)
            reduce(R_BLOCK + HEADS - 1, 4)
            with pe.Fori(0, PAIRS) as i:
                over_model(U_M, 0, col_hi, col_lo, i, 8)
                over_model(U_M + 4, 2, br_hi, br_lo, i, 8)
            for q in range(NQ):
                pe.wait_ge(mg_lo, 2 * (q + 1))
                over_model(U_O, 0, col_hi, col_lo, qs=(q,))
            over_model(U_O + 4, 2, col_hi, col_lo)
            with pe.Fori(0, 3) as i:
                over_model(U_O + 8, 0, col_hi, col_lo, i, 8)
                over_model(U_O + 12, 2, col_hi, col_lo, i, 8)
            position_sums(PAIRS, 4, sum2)
            pe.wait_ge(rstd_cast, 2)
            spread(5)
            for q in range(NQ):
                for p in range(4):
                    if q == 0 and p == 0:
                        products(U_F, banks(0), *tiles(col_hi, col_lo, 0), stop=False, tile_ready=h2_lo)
                        continue
                    if p == 0:
                        pe.wait_ge(h2_lo, QT * (q + 1))
                    products(U_F + 4 * q + p, banks(2 * p), *tiles(col_hi, col_lo, q), start=q == 0, stop=q == NQ - 1)

            def down(u, d, i=None):
                if d >= 2:
                    base_ = 0 if i is not None else 8 * (GROUPS - 1)
                    pe.wait_ge(down_added, base_ + d - 1 if i is None else i * 8 + (d - 1))
                products(u + d, banks(4 + 2 * (d % 2)), lambda k: u_hi[:, k], lambda k: u_lo[:, k], i=i, n=F_SEG)

            with pe.Fori(0, GROUPS - 1) as i:
                over_model(U_L, 0, col_hi, col_lo, i, F_SEG)
                pe.wait_ge(u_lo_ready, i * 2 + 2)
                for d in range(8):
                    down(U_L + 4, d, i)
                over_model(U_L + 12, 2, col_hi, col_lo, i, F_SEG)
                over_model(U_L + 16, 4, col_hi, col_lo, i, F_SEG)
                over_model(U_L + 20, 6, col_hi, col_lo, i, F_SEG)

            def turn(d):
                pe.wait_ge(scaled_ready, d + 1)
                if d >= 2:
                    pe.wait_ge(rows_ready, d - 1)
                for s in range(ST):
                    for m in range(2):
                        o = ps[:, 2 * (d % 2) + s // 2, (s % 2) * UC + m * P:(s % 2) * UC + (m + 1) * P]
                        mm = pe.transpose(o, scaled[:, d % 2, m, s * P:(s + 1) * P], ident[:])
                mm.then_inc(turned, 1)

            for half in range(2):
                pe.wait_ge(u_lo_ready, 2 * GROUPS - 1 + half)
                for d in range(2):
                    products(U_D + d, banks((4, 2)[d]), lambda k: u_hi[:, k], lambda k: u_lo[:, k],
                             ks=range(2 * half, 2 * half + 2), start=half == 0, stop=half == 1, last=half == 1)
            for d in range(2, 8):
                down(U_D, d)
                turn(d - 2)
            turn(6)
            turn(7)
            position_sums(2 * PAIRS, 4, sum3)

        @block.scalar
        def _(act):
            def split(u, i=None, n=0, extra=0, extra_n=0):
                need = 16 * (u // RAW + 1 + extra)
                act.wait_ge(w_loaded[u % RAW], need if i is None else i * (16 * (n // RAW + extra_n)) + need)
                if u >= SPLIT:
                    act.wait_ge(unit_done, u - 1 if i is None else i * n + (u - 1))
                act.activation(w_hi[:, u % SPLIT], w_raw[:, u % RAW], ACT.Copy).then_inc(hi_made, 1)

            def split_range(us, extra=0):
                for u in us:
                    split(u, extra=extra)

            def feed(seg, quarter, i=None, segs=0):
                for t in range(STAGE * quarter, STAGE * (quarter + 1)):
                    start = (LATER + seg) * MC if i is None else act.snap(i * (segs * MC) + (LATER + seg) * MC)
                    if seg or quarter:
                        done = NT * seg + t - STAGE + 1
                        act.wait_ge(mac, done if i is None else i * (segs * NT) + done)
                    act.dma_start(ada_stage[:, t % STAGE], ada_v[:, t, span(start, MC)]).then_inc(ada_in[t % STAGE], 16)

            def biased(outs, b, func, name, tile, sem_, count=2):
                for m in range(count):
                    a_ = act.activation(outs[m], ps[:, b + m], func, bias=col(name, tile + m), scale=1.0)
                a_.then_inc(sem_, 1)

            act.wait_ge(par_ready, 1)
            act.activation(small["cact"][:], col("c", 0, NT), ACT.Sigmoid).then_inc(sig_c, 1)
            for s in range(ST):
                act.wait_ge(x_in[s], 16)
                a_ = act.activation(square_out[:], x_rows[:, s], ACT.Square, accum_out=row_sq[:, s:s + 1])
                a_.then_inc(sq_rows, 1)
                if s < ST - 1:
                    act.wait_ge(sq_rows, s + 1)
            act.wait_ge(rstd_rows, 1)
            act.activation(row_rstd[:], row_rstd[:], ACT.Sqrt).then_inc(std_rows, 1)
            for t in range(NT):
                act.wait_ge(x_turned, t + 1)
                act.activation(xT[:, t], ps[:, t % 4], ACT.Copy).then_inc(xT_ready, 1)
            split(0)
            split(1)

            def h_quarter(q):
                act.wait_ge(mod0_ready, 2 * (q + 1))
                act.wait_ge(xn_ready, QT * (q + 1))
                for t in range(QT * q, QT * (q + 1)):
                    a_ = act.activation(xn[:, t], xn[:, t], ACT.Identity, bias=mod[:, SH1 + t:SH1 + t + 1],
                                        scale=small["gain1"][:, t:t + 1])
                a_.then_inc(h_ready, 1)
                act.wait_ge(h_ready, q + 1)
                act.activation(col_hi[:, QT * q:QT * (q + 1)], xn[:, QT * q:QT * (q + 1)], ACT.Copy).then_inc(h_hi, 1)

            for q in range(NQ):
                h_quarter(q)
                if q < NQ - 1:
                    split_range(range(3 * q + 2, 3 * q + 5))

            def pool_in(p, b):
                if p == 0:
                    act.wait_ge(pads_ready, 2)
                else:
                    act.wait_ge(pool_f, p)
                biased([z[:, m, PAD:] for m in range(2)], b, ACT.Identity, "b_in", XP + 2 * p, z_ready)
                act.wait_ge(pool_f, p + 1)
                act.activation(pool_hi[:, 2 * p:2 * p + 2], win_of(p)[:, :, PAD:], ACT.Copy).then_inc(pool_hi_ready, 1)

            for p in range(3):
                split(9 + p + 2)
                pool_in(p, 2 * p)
            def position(u, extra=0):
                split(u + 2)
                for seg in range(EARLY):
                    if u in EARLY_FEED[seg]:
                        feed(seg, EARLY_FEED[seg].index(u))

            for u in range(U_P3, U_GB0):
                position(u)
            pool_in(3, 6)
            for u in range(U_GB0, U_PW):
                position(u)
            act.wait_ge(rate_in, 1)
            act.activation(small["sig_l"][:], small["lam_abs"][:], ACT.Sigmoid, scale=-1.0).then_inc(lam_sig, 1)
            biased([gate_b[:, 0, m] for m in range(2)], 0, ACT.Sigmoid, "b_in", GB, gate_ready)
            for k in range(2):
                position(U_PW + k)
                for g in (2 * k, 2 * k + 1):
                    act.wait_ge(yb_f, g + 1)
                    act.activation(yb_hi[:, 2 * g:2 * g + 2], ybf[:], ACT.Copy).then_inc(yb_hi_ready, 1)
            for u in range(U_GB1, U_B):
                position(u)
            biased([gate_b[:, 1, m] for m in range(2)], 2, ACT.Sigmoid, "b_in", GB + 2, gate_ready)

            def store_pb(j, i=None):
                start = 2 * j if i is None else act.snap(i * 4 + 2 * j)
                act.wait_ge(pb_made, j + 1 if i is None else i * 2 + (j + 1))
                act.dma_start(pool_spill[:, span(start, 2)], pbf[:]).then_inc(spilled, 16)

            with act.Fori(0, B_TURNS) as i:
                for half in range(2):
                    for k in range(B_SEG):
                        split(U_B + half * B_SEG + k + 2, i, 2 * B_SEG)
                        if k == 2:
                            store_pb(half, i)
                        if k in B_FEED:
                            feed(EARLY + half, B_FEED.index(k), i, 2)
                        if k == 5:
                            biased([gate_b[:, half, m] for m in range(2)], 0, ACT.Sigmoid, "b_in",
                                   i * 4 + (2 * half + GB + 4), gate_ready)
            for k in range(4):
                split(U_B2 + k + 2)
                if k % 2:
                    store_pb(2 * B_TURNS + k // 2)

            with act.Fori(0, R_TURNS) as i:
                n = R_SEG * R_HEADS
                for head in range(R_HEADS):
                    seg, tile = R_BLOCK + head, i * (2 * R_HEADS) + 2 * head
                    nth = i * R_HEADS + (head + 1)
                    for k in range(R_SEG):
                        u = U_R + head * R_SEG + k + 2
                        split(u, i, n, *lru_extra(u))
                        if k in R_FEED:
                            feed(seg, R_FEED.index(k), i, R_HEADS)
                        if k == 3:
                            biased([z[:, m, PAD:] for m in range(2)], 0, ACT.Identity, "b_in", tile, z_ready)
                            act.wait_ge(xr_ready, nth)
                            act.activation(xr_hi[:], xr[:], ACT.Copy).then_inc(xr_hi_ready, 1)
                        if k == 6:
                            biased([decay[:, m] for m in range(2)], 4, ACT.Sigmoid, "ba", tile, r_ready)
                            biased([inp[:, m] for m in range(2)], 6, ACT.Sigmoid, "bx", tile, gates_ready)
                            act.wait_ge(gates_ready, nth)
                            for m in range(2):
                                a_ = act.activation(tanh_q[:, m], decay[:, m], ACT.Tanh, scale=cols(small["rate"], tile + m))
                            a_.then_inc(tanh_ready, 1)
                        if k == 7:
                            act.wait_ge(tanh_ready, nth)
                            for m in range(2):
                                a_ = act.activation(decay[:, m], decay[:, m], ACT.Exp, scale=cols(small["neg_rate"], tile + m))
                            a_.then_inc(decay_ready, 1)
                            act.wait_ge(decay_ready, nth)
                            act.activation(z[:, :, PAD:], decay[:], ACT.Square).then_inc(decay_sq, 1)
                        if k == 8:
                            act.wait_ge(var_ready, nth)
                            act.activation(tanh_q[:], tanh_q[:], ACT.Sqrt).then_inc(root_ready, 1)
                            biased([gelu[:, m] for m in range(2)], 2, ACT.Gelu_apprx_tanh, "b_in", tile + GT, gelu_ready)
                            act.wait_ge(ya_f, nth)
                            act.activation(br_hi[:, bass.ds(act.snap(tile), 2)], gelu[:], ACT.Copy).then_inc(ya_hi_ready, 1)

            with act.Fori(0, PAIRS) as i:
                for k in range(8):
                    split(U_M + k + 2, i, 8, TWO)
                    if k == 2:
                        act.dma_start(pb_in[:], pool_spill[:, bass.ds(act.snap(i * 2), 2)]).then_inc(pb_back, 16)
                    if k == 3:
                        biased([gate_a[:, m] for m in range(2)], 0, ACT.Sigmoid, "b_in", i * 2 + GA, gate_ready)

            def merge_hi(d):
                act.wait_ge(merged_ready, d + 1)
                act.activation(col_hi[:, 2 * d:2 * d + 2], merged[:, 2 * d:2 * d + 2], ACT.Copy).then_inc(mg_hi, 1)

            def squares(d, i=None, count=None):
                start = 2 * d if i is None else act.snap(i * 4 + 2 * d)
                act.wait_ge(x2_ready, d + 1 if i is None else i * 2 + (d + 1))
                act.activation(sq[:], resid[:, span(start, 2)], ACT.Square).then_inc(sq_ready, 1)

            merge_hi(0)
            merge_hi(1)
            for k in range(8):
                if k < 3:
                    merge_hi(2 * k + 2)
                    merge_hi(2 * k + 3)
                split(U_O + k + 2, extra=TWO)
                if k % 4 == 3:
                    squares(k // 4)
            with act.Fori(0, 3) as i:
                for half in range(2):
                    for k in range(4):
                        split(U_O + 8 + half * 4 + k + 2, i, 8, TWO)
                        if k == 3:
                            squares(half + 2, i)
            act.wait_ge(var2, 1)
            act.activation(row_rstd[:], row_rstd[:], ACT.Sqrt).then_inc(std2, 1)

            def h2_tile(t):
                act.wait_ge(xn2_ready, t + 1)
                act.activation(h2f[:, t % QT], h2f[:, t % QT], ACT.Identity, bias=mod[:, SH2 + t:SH2 + t + 1],
                               scale=small["gain2"][:, t:t + 1]).then_inc(h2_ready, 1)
                act.wait_ge(h2_ready, t + 1)
                act.activation(col_hi[:, t], h2f[:, t % QT], ACT.Copy).then_inc(h2_hi, 1)

            def conv_post(pair, b, nth, i, g4):
                buf = conv_l if pair % 2 else conv_a
                if pair >= 2:
                    act.wait_ge(u_lo_ready if pair % 2 else silu_ready, 1 if i is None else i * 2 + 3)
                for m in range(2):
                    tile = (2 * (pair // 2) + m + (pair % 2) * (DF // P)) + g4
                    a_ = act.activation(buf[:, m], ps[:, b + m], ACT.Identity, bias=col("ffn_b", tile), scale=col("ffn_w2", tile))
                a_.then_inc(tap_ready, 1)
                act.wait_ge(conv_ready, nth)
                if pair % 2 == 0:
                    act.activation(silu_a[:, pair // 2], conv_a[:], ACT.Silu).then_inc(silu_ready, 1)

            def u_high(pair, nth):
                act.wait_ge(uf_ready, nth)
                k = pair // 2
                act.activation(u_hi[:, 2 * k:2 * k + 2], conv_l[:], ACT.Copy).then_inc(u_hi_ready, 1)

            for t in range(QT):
                h2_tile(t)
            for k in range(16):
                if k + QT < NT:
                    h2_tile(k + QT)
                split(U_F + k + 2, extra=TWO)
                if k >= 12:
                    pair = k - 12
                    conv_post(pair, 2 * pair, pair + 1, None, 0)
                    if pair % 2:
                        u_high(pair, pair // 2 + 1)
            with act.Fori(0, GROUPS - 1) as i:
                for k in range(F_SEG):
                    split(U_L + k + 2, i, F_SEG, TWO)
                    if k in (3, 15, 19, 23):
                        pair = (3, 15, 19, 23).index(k)
                        conv_post(pair, 2 * pair, i * 4 + (5 + pair), i, i * QT + QT)
                        if pair % 2:
                            u_high(pair, i * 2 + (3 + pair // 2))

            def copy_rows(d):
                act.wait_ge(turned, d + 1)
                src = ps[:, 2 * (d % 2):2 * (d % 2) + 2].rearrange("p b (s c) -> p (b s) c", s=2)
                act.activation(rows_out[:, :, d * UC:(d + 1) * UC], src, ACT.Copy).then_inc(rows_ready, 1)

            for d in range(8):
                if U_D + d + 2 < UNITS:
                    split(U_D + d + 2, extra=TWO)
                act.wait_ge(down_added, 8 * (GROUPS - 1) + d + 1)
                act.activation(sq[:], resid[:, 2 * d:2 * d + 2], ACT.Square).then_inc(sq_ready, 1)
                if d >= 2:
                    act.wait_ge(turned, d - 1)
                for m in range(2):
                    t = 2 * d + m
                    a_ = act.activation(scaled[:, d % 2, m], resid[:, t], ACT.Copy, scale=col("g_out", t))
                a_.then_inc(scaled_ready, 1)
                if d >= 2:
                    copy_rows(d - 2)
            copy_rows(6)
            copy_rows(7)
            act.wait_ge(var3, 1)
            act.activation(row_rstd[:], row_rstd[:], ACT.Sqrt).then_inc(std3, 1)
            act.wait_ge(rstd3, 1)
            for s in range(1, ST, 2):
                act.activation(rows_out[:, s], rows_out[:, s], ACT.Copy, scale=row_rstd[:, s:s + 1]).then_inc(rows_act, 1)

        @block.vector
        def _(v):
            own = Steps(steps_v)

            def split(u, i=None, n=0):
                v.wait_ge(hi_made, u + 1 if i is None else i * n + (u + 1))
                v.tensor_tensor(w_lo[:, u % SPLIT], w_raw[:, u % RAW], w_hi[:, u % SPLIT].bitcast(F32), ALU.subtract
                                ).then_inc(lo_made, 1)

            def low(out_, full, high, sem_):
                v.tensor_tensor(out_, full, high.bitcast(F32), ALU.subtract).then_inc(sem_, 1)

            v.wait_ge(par_turned, 1)
            for n in range(NP):
                last = v.tensor_copy(par[:, n * P:n * P + pack_rows[n]], ps[:, 6 + n // 4, (n % 4) * P:(n % 4) * P + pack_rows[n]])
            last.then_inc(par_ready, 1)
            v.wait_ge(par_ready, 1)
            v.wait_ge(sig_c, 1)
            v.wait_ge(const_ready, 3)
            cact = small["cact"]
            v.tensor_tensor(cact[:], cact[:], col("c", 0, NT), ALU.mult).then_inc(cact_ready, 1)
            v.wait_ge(cact_ready, 1)

            def mac_chunk0(n):
                b, k = n // CH, n % CH
                acc = ada_acc0[:, b % 2]
                v.wait_ge(ada0_in[n % STAGE0], 16 * (n // STAGE0 + 1))
                if k == 0 and b >= 2:
                    v.wait_ge(reduced0, b - 1)
                for r in range(CHUNK):
                    t = k * CHUNK + r
                    w = ada_stage0[:, n % STAGE0, r]
                    if t == 0:
                        v.tensor_scalar(acc, w, cact[:, 0:1], None, ALU.mult).then_inc(mac0, 1)
                    else:
                        v.wait_ge(mac0, NT * b + t)
                        v.scalar_tensor_tensor(acc, w, cact[:, t:t + 1], acc, ALU.mult, ALU.add).then_inc(mac0, 1)

            def mod0(b):
                v.wait_ge(reduced0, b + 1)
                t = first_blocks[b] * QT
                if b % 2 == 0:
                    own.done(v.tensor_tensor(mod[:, t:t + QT], ps[:, 7, b * QT:(b + 1) * QT], col("ada_b", t, QT), ALU.add))
                    own.wait(v)
                    k = t - SC1
                    v.scalar_tensor_tensor(small["gain1"][:, k:k + QT], mod[:, t:t + QT], 1.0, col("g_mix", k, QT),
                                           ALU.add, ALU.mult).then_inc(mod0_ready, 1)
                else:
                    v.tensor_tensor(mod[:, t:t + QT], ps[:, 7, b * QT:(b + 1) * QT], col("ada_b", t, QT), ALU.add
                                    ).then_inc(mod0_ready, 1)

            def widen_rstd():
                own.done(v.reciprocal(row_rstd[:], row_rstd[:]))
                own.wait(v)
                for s in range(ST):
                    last = v.tensor_scalar(rstd_wide[:, s], ones[:], row_rstd[:, s:s + 1], None, ALU.mult)
                last.then_inc(rstd_cast, 1)

            def h_low(q):
                v.wait_ge(h_hi, q + 1)
                low(col_lo[:, QT * q:QT * (q + 1)], xn[:, QT * q:QT * (q + 1)], col_hi[:, QT * q:QT * (q + 1)], h_lo)

            for n in range(QC * NQ):
                mac_chunk0(n)
                if n == 7:
                    v.wait_ge(sq_rows, ST)
                    v.tensor_scalar(row_rstd[:], row_sq[:], 1.0 / D, EPS, ALU.mult, ALU.add).then_inc(rstd_rows, 1)
                if n == 9:
                    v.wait_ge(std_rows, 1)
                    widen_rstd()
                if n == 11:
                    v.wait_ge(rstd_spread, 1)
                    v.tensor_copy(rstd_bc[:], ps[:, 6]).then_inc(rstd_ready, 1)
                if n == SPLIT_FIRST:
                    split(0)
                    split(1)
                if n % CH == 2 and n > CH:
                    mod0(n // CH - 1)
                if n in h_lo_due:
                    h_low(h_lo_due[n])
                if n in split_due:
                    split(split_due[n])
            mod0(2 * NQ - 1)
            for n in sorted(split_due):
                if n >= QC * NQ:
                    split(split_due[n])
            h_low(NQ - 1)

            def pool_windows(p):
                v.wait_ge(z_ready, p + 1)
                if p:
                    v.wait_ge(pool_lo_ready, p)
                src, step, bufs = z, 1, (win_a, win_b)
                for r in range(p + 1):
                    dst = bufs[r % 2]
                    lo_ = 2 * step - 1
                    own.done(v.tensor_tensor(dst[:, :, lo_:], src[:, :, lo_:], src[:, :, lo_ - step:PAD + S - step], ALU.add))
                    own.wait(v)
                    src, step = dst, 2 * step
                own.done(v.tensor_tensor(src[:, :, PAD:2 * PAD], src[:, :, PAD:2 * PAD], count_fix[:, p], ALU.mult))
                own.wait(v)
                assert src is win_of(p)
                v.scalar_tensor_tensor(src[:, :, PAD:], src[:, :, PAD:], 1.0 / WINDOWS[p], z[:, :, PAD:], ALU.mult,
                                       ALU.subtract).then_inc(pool_f, 1)
                v.wait_ge(pool_hi_ready, p + 1)
                low(pool_lo[:, 2 * p:2 * p + 2], src[:, :, PAD:], pool_hi[:, 2 * p:2 * p + 2], pool_lo_ready)

            def macs(seg, quarter, i=None, segs=0):
                for t in range(STAGE * quarter, STAGE * (quarter + 1)):
                    need = 16 * (NT // STAGE * seg + quarter + 1)
                    v.wait_ge(ada_in[t % STAGE], need if i is None else i * (16 * (NT // STAGE) * segs) + need)
                    w = ada_stage[:, t % STAGE]
                    if t == 0:
                        v.tensor_scalar(ada_acc[:], w, cact[:, 0:1], None, ALU.mult).then_inc(mac, 1)
                    else:
                        so_far = NT * seg + t
                        v.wait_ge(mac, so_far if i is None else i * (segs * NT) + so_far)
                        v.scalar_tensor_tensor(ada_acc[:], w, cact[:, t:t + 1], ada_acc[:], ALU.mult, ALU.add
                                               ).then_inc(mac, 1)

            def modulation(seg, bank, i=None, segs=0):
                t = (LATER + seg) * QT if i is None else v.snap(i * (segs * QT) + (LATER + seg) * QT)
                tb = (LATER + seg) * QT if i is None else i * (segs * QT) + (LATER + seg) * QT
                v.wait_ge(reduced, seg + 1 if i is None else i * segs + (seg + 1))
                v.tensor_tensor(mod[:, span(t, QT)], ps[:, bank, 0:QT], col("ada_b", tb, QT), ALU.add).then_inc(mod_ready, 1)

            def position(u):
                split(u + 2)
                for seg in range(EARLY):
                    if u in EARLY_SUM[seg]:
                        macs(seg, EARLY_SUM[seg].index(u))
                if u == U_GB0 + 2:
                    modulation(0, 7)

            for p in range(3):
                split(9 + p + 2)
                pool_windows(p)
            for u in range(U_P3, U_GB0):
                position(u)
            pool_windows(3)
            sm = small

            def step_(ins):
                own.done(ins)
                own.wait(v)

            step_(v.tensor_scalar(sm["lam_neg"][:], col("lam", 0, NT), -1.0, None, ALU.mult))
            v.tensor_tensor(sm["lam_abs"][:], sm["lam_neg"][:], col("lam", 0, NT), ALU.max).then_inc(rate_in, 1)
            for u in range(U_GB0, U_PW):
                position(u)
            v.wait_ge(lam_sig, 1)
            step_(v.tensor_scalar(sm["ser_p"][:], sm["sig_l"][:], -1.0, 2.0, ALU.mult, ALU.add))
            step_(v.reciprocal(sm["ser_s"][:], sm["ser_p"][:]))
            step_(v.tensor_tensor(sm["ser_s"][:], sm["ser_s"][:], sm["sig_l"][:], ALU.mult))
            step_(v.tensor_tensor(sm["ser_s2"][:], sm["ser_s"][:], sm["ser_s"][:], ALU.mult))
            step_(v.tensor_scalar(sm["ser_p"][:], sm["ser_s2"][:], 1.0 / 17, None, ALU.mult))
            for odd in (15, 13, 11, 9, 7, 5, 3):
                step_(v.scalar_tensor_tensor(sm["ser_p"][:], sm["ser_p"][:], 1.0 / odd, sm["ser_s2"][:], ALU.add, ALU.mult))
            step_(v.scalar_tensor_tensor(sm["ser_p"][:], sm["ser_p"][:], 1.0, sm["ser_s"][:], ALU.add, ALU.mult))
            step_(v.tensor_scalar(sm["lam_neg"][:], sm["lam_neg"][:], 0.0, None, ALU.max))
            step_(v.scalar_tensor_tensor(sm["rate"][:], sm["ser_p"][:], 2.0, sm["lam_neg"][:], ALU.mult, ALU.add))
            step_(v.tensor_scalar(sm["neg_rate"][:], sm["rate"][:], -LRU_C, None, ALU.mult))
            v.tensor_scalar(sm["rate"][:], sm["rate"][:], LRU_C, None, ALU.mult).then_inc(rate_ready, 1)

            for k in range(2):
                position(U_PW + k)
                for g in (2 * k, 2 * k + 1):
                    if g:
                        v.wait_ge(yb_lo_ready, g)
                    for m in range(2):
                        last = v.tensor_scalar(ybf[:, m], ps[:, (2, 4, 6, 0)[g] + m], col("pool_b", 2 * g + m),
                                               col("pool_s", 2 * g + m), ALU.add, ALU.mult)
                    last.then_inc(yb_f, 1)
                    v.wait_ge(yb_hi_ready, g + 1)
                    low(yb_lo[:, 2 * g:2 * g + 2], ybf[:], yb_hi[:, 2 * g:2 * g + 2], yb_lo_ready)
            for u in range(U_GB1, U_B):
                position(u)

            def share_b(j, i=None, b=4):
                v.wait_ge(gate_ready, j + 1 if i is None else i * 2 + (j + 1))
                v.wait_ge(spilled, 16 * (j + 1) if i is None else i * 32 + 16 * (j + 1))
                v.tensor_tensor(pbf[:], ps[:, b:b + 2], gate_b[:, j % 2], ALU.mult).then_inc(pb_made, 1)

            with v.Fori(0, B_TURNS) as i:
                for half in range(2):
                    for k in range(B_SEG):
                        split(U_B + half * B_SEG + k + 2, i, 2 * B_SEG)
                        if k == 1:
                            share_b(half, i)
                            modulation(EARLY + half - 1, 7, i, 2)
                        if k - 1 in B_FEED:
                            macs(EARLY + half, B_FEED.index(k - 1), i, 2)
            for k in range(4):
                split(U_B2 + k + 2)
                if k % 2:
                    share_b(2 * B_TURNS + k // 2, b=(4, 2)[k // 2])

            with v.Fori(0, R_TURNS) as i:
                n = R_SEG * R_HEADS
                own.loop(i, R_HEADS * (TAPS - 1 + 3))
                for head in range(R_HEADS):
                    seg, tile = R_BLOCK + head, i * (2 * R_HEADS) + 2 * head
                    nth = i * R_HEADS + (head + 1)
                    for k in range(R_SEG):
                        split(U_R + head * R_SEG + k + 2, i, n)
                        if k == 1:
                            modulation(seg - 1, 4, i, R_HEADS)
                        if k in R_SUM:
                            macs(seg, R_SUM.index(k), i, R_HEADS)
                        if k == 3:
                            v.wait_ge(z_ready, i * R_HEADS + (head + 1 + len(WINDOWS)))
                            for tap in range(TAPS):
                                w_at = tile + (TAPS - 1 - tap) * NT
                                for m in range(2):
                                    src = z[:, m, PAD - tap:PAD + S - tap]
                                    if tap == 0:
                                        last = v.tensor_scalar(xr[:, m], src, col("conv_w", w_at + m), col("conv_b", tile + m),
                                                               ALU.mult, ALU.add)
                                    else:
                                        last = v.scalar_tensor_tensor(xr[:, m], src, col("conv_w", w_at + m), xr[:, m],
                                                                      ALU.mult, ALU.add)
                                if tap < TAPS - 1:
                                    step_(last)
                            last.then_inc(xr_ready, 1)
                            v.wait_ge(xr_hi_ready, nth)
                            low(xr_lo[:], xr[:], xr_hi[:], xr_lo_ready)
                        if k == 6:
                            v.wait_ge(gates_ready, nth)
                            step_(v.tensor_tensor(inp[:], inp[:], xr[:], ALU.mult))
                        if k == 7:
                            v.wait_ge(decay_sq, nth)
                            v.scalar_tensor_tensor(tanh_q[:], z[:, :, PAD:], 1.0, tanh_q[:], ALU.add, ALU.mult
                                                   ).then_inc(var_ready, 1)
                        if k == 8:
                            v.wait_ge(root_ready, nth)
                            step_(v.tensor_tensor(inp[:], inp[:], tanh_q[:], ALU.mult))
                            for m in range(2):
                                last = v.tensor_tensor_scan(z[:, m, PAD:], decay[:, m], inp[:, m], 0.0, ALU.mult, ALU.add)
                            step_(last)
                            v.wait_ge(gelu_ready, nth)
                            v.tensor_tensor(gelu[:], z[:, :, PAD:], gelu[:], ALU.mult).then_inc(ya_f, 1)
                            v.wait_ge(ya_hi_ready, nth)
                            ts = bass.ds(v.snap(tile), 2)
                            low(br_lo[:, ts], gelu[:], br_hi[:, ts], ya_lo_ready)
                own.end(R_TURNS)
            modulation(R_BLOCK + HEADS - 1, 4)
            v.wait_ge(mod_ready, R_BLOCK + HEADS)
            step_(v.scalar_tensor_tensor(sm["gain2"][:], mod[:, SC2:SC2 + NT], 1.0, col("g_ffn", 0, NT), ALU.add, ALU.mult))

            with v.Fori(0, PAIRS) as i:
                own.loop(i, 1)
                for k in range(8):
                    split(U_M + k + 2, i, 8)
                    if k == 7:
                        v.wait_ge(gate_ready, i + (PAIRS + 1))
                        step_(v.tensor_tensor(gate_a[:], ps[:, 2:4], gate_a[:], ALU.mult))
                        v.wait_ge(pb_back, i * 16 + 16)
                        v.tensor_tensor(merged[:, bass.ds(v.snap(i * 2), 2)], gate_a[:], pb_in[:], ALU.add
                                        ).then_inc(merged_ready, 1)
                own.end(PAIRS)

            def merge_lo(d):
                v.wait_ge(mg_hi, d + 1)
                low(col_lo[:, 2 * d:2 * d + 2], merged[:, 2 * d:2 * d + 2], col_hi[:, 2 * d:2 * d + 2], mg_lo)

            def add_squares(count):
                v.wait_ge(sq_ready, count)
                if not isinstance(count, int) or count > 1:
                    v.wait_ge(sq_used, count - 1)
                step_(v.tensor_tensor(sq_sum[:], sq_sum[:], sq[:, 0], ALU.add))
                v.tensor_tensor(sq_sum[:], sq_sum[:], sq[:, 1], ALU.add).then_inc(sq_used, 1)

            def add_out(d, b, i=None):
                tile = 2 * d if i is None else i * 4 + 2 * d
                for m in range(2):
                    r = resid[:, 2 * d + m] if i is None else resid[:, bass.ds(v.snap(tile + m), 1)].rearrange("p a s -> p (a s)")
                    last = v.scalar_tensor_tensor(r, ps[:, b + m], cols(mod, tile + (GT1 + m)), r, ALU.mult, ALU.add)
                last.then_inc(x2_ready, 1)
                add_squares(d + 1 if i is None else i * 2 + (d + 1))

            merge_lo(0)
            merge_lo(1)
            for k in range(8):
                if k < 3:
                    merge_lo(2 * k + 2)
                    merge_lo(2 * k + 3)
                if k == 3:
                    step_(v.memset(sq_sum[:], 0.0))
                split(U_O + k + 2)
                if k % 4 == 3:
                    v.wait_ge(resid_in[0], 16)
                    add_out(k // 4, 2 * (k // 4))
            for q in range(1, NQ):
                v.wait_ge(resid_in[q], 16)
            with v.Fori(0, 3) as i:
                own.loop(i, 2)
                for half in range(2):
                    for k in range(4):
                        split(U_O + 8 + half * 4 + k + 2, i, 8)
                        if k == 3:
                            add_out(half + 2, 2 * half, i)
                own.end(3)
            v.wait_ge(sum2, 1)
            v.tensor_scalar(row_rstd[:], ps[:, 4, 0:ST], 1.0 / D, EPS, ALU.mult, ALU.add).then_inc(var2, 1)
            v.wait_ge(std2, 1)
            widen_rstd()
            v.wait_ge(rstd_spread, 2)
            v.tensor_copy(rstd_bc[:], ps[:, 5]).then_inc(rstd_ready, 1)
            v.wait_ge(rstd_ready, 2)

            def xn2(t):
                if t >= QT:
                    v.wait_ge(h2_lo, t - QT + 1)
                v.tensor_tensor(h2f[:, t % QT], resid[:, t], rstd_bc[:], ALU.mult).then_inc(xn2_ready, 1)

            def h2_low(t):
                v.wait_ge(h2_hi, t + 1)
                low(col_lo[:, t], h2f[:, t % QT], col_hi[:, t], h2_lo)

            def conv_taps(pair, b, nth, g4):
                buf = conv_l if pair % 2 else conv_a
                v.wait_ge(tap_ready, nth)
                for tap in (1, 2):
                    for m in range(2):
                        tile = (2 * (pair // 2) + m + (pair % 2) * (DF // P)) + g4
                        last = v.scalar_tensor_tensor(buf[:, m, tap:], ps[:, b + m, 0:S - tap],
                                                      col("ffn_w1" if tap == 1 else "ffn_w0", tile), buf[:, m, tap:],
                                                      ALU.mult, ALU.add)
                    if tap == 1:
                        step_(last)
                last.then_inc(conv_ready, 1)

            def make_u(pair, nth_conv, nth_silu, nth):
                k = pair // 2
                v.wait_ge(conv_ready, nth_conv)
                v.wait_ge(silu_ready, nth_silu)
                v.tensor_tensor(conv_l[:], silu_a[:, k], conv_l[:], ALU.mult).then_inc(uf_ready, 1)
                v.wait_ge(u_hi_ready, nth)
                low(u_lo[:, 2 * k:2 * k + 2], conv_l[:], u_hi[:, 2 * k:2 * k + 2], u_lo_ready)

            def add_down(d, b=None):
                b = 4 + 2 * (d % 2) if b is None else b
                for m in range(2):
                    t = 2 * d + m
                    last = v.scalar_tensor_tensor(resid[:, t], ps[:, b + m], mod[:, GT2 + t:GT2 + t + 1],
                                                  resid[:, t], ALU.mult, ALU.add)
                last.then_inc(down_added, 1)

            xn2(0)
            for t in range(QT):
                if t + 1 < QT:
                    xn2(t + 1)
                h2_low(t)
            for k in range(16):
                if k + QT < NT:
                    xn2(k + QT)
                    h2_low(k + QT)
                split(U_F + k + 2)
                if k >= 12:
                    pair = k - 12
                    conv_taps(pair, 2 * pair, pair + 1, 0)
                    if pair % 2:
                        make_u(pair, pair + 1, pair // 2 + 1, pair // 2 + 1)
            with v.Fori(0, GROUPS - 1) as i:
                own.loop(i, 4)
                for k in range(F_SEG):
                    split(U_L + k + 2, i, F_SEG)
                    if 4 <= k < 12:
                        add_down(k - 4)
                    if k in (3, 15, 19, 23):
                        pair = (3, 15, 19, 23).index(k)
                        conv_taps(pair, 2 * pair, i * 4 + (5 + pair), i * QT + QT)
                        if pair % 2:
                            make_u(pair, i * 4 + (5 + pair), i * 2 + (3 + pair // 2), i * 2 + (3 + pair // 2))
                own.end(GROUPS - 1)
            step_(v.memset(sq_sum[:], 0.0))
            for d in range(8):
                if U_D + d + 2 < UNITS:
                    split(U_D + d + 2)
                v.wait_ge(unit_done, U_D + d + 1)
                add_down(d, 2 if d == 1 else None)
                add_squares(PAIRS + d + 1)
            v.wait_ge(sum3, 1)
            v.tensor_scalar(row_rstd[:], ps[:, 4, 0:ST], 1.0 / D, EPS, ALU.mult, ALU.add).then_inc(var3, 1)
            v.wait_ge(std3, 1)
            v.reciprocal(row_rstd[:], row_rstd[:]).then_inc(rstd3, 1)
            v.wait_ge(rstd3, 1)
            for s in range(0, ST, 2):
                v.tensor_scalar(rows_out[:, s], rows_out[:, s], row_rstd[:, s:s + 1], None, ALU.mult).then_inc(rows_dve, 1)


_INS = ['x', 'c', 'ada_w', 'ada_b', 'norm_mix_g', 'w_in', 'b_in', 'conv_w', 'conv_b', 'lru_wa', 'lru_ba', 'lru_wx',
        'lru_bx', 'lru_lambda', 'pool_w', 'pool_b', 'pool_scale', 'proj_a', 'proj_b', 'w_out', 'norm_ffn_g', 'w_up',
        'ffn_conv_w', 'ffn_conv_b', 'w_down', 'final_g']
_OUTS = [((1, 512, 2048), 'float32')]


def kernel(**inputs):
    import numpy as _np
    import concourse.bacc as _bacc
    from concourse import mybir as _mybir
    from concourse.bass_utils import run_bass_kernel_spmd as _run

    nc = _bacc.Bacc("TRN2", target_bir_lowering=False, num_devices=1)
    arrays, args = {}, []
    for name in _INS:
        a = _np.ascontiguousarray(inputs[name])
        arrays[f"in_{name}_dram"] = a
        args.append(nc.dram_tensor(f"in_{name}_dram", a.shape, _mybir.dt.from_np(a.dtype), kind="ExternalInput").ap())
    for i, (shape, dtype) in enumerate(_OUTS):
        dt = _mybir.dt.from_np(_np.dtype(dtype))
        args.append(nc.dram_tensor(f"out_{i}_dram", shape, dt, kind="ExternalOutput").ap())
    trunk_kernel(nc, *args)
    r = _run(nc, [arrays], core_ids=[0])
    got = tuple(r.results[0][f"out_{i}_dram"] for i in range(len(_OUTS)))
    return got[0]
```

```python
import concourse.bass as bass
from concourse import mybir
from contextlib import ExitStack

F32 = mybir.dt.float32
F32R = mybir.dt.float32r
ALU = mybir.AluOpType
ACT = mybir.ActivationFunctionType

P = 128
KB = 1024
QT = 4
UC = 256
EPS = 1e-6
LRU_C = 8.0
WINDOWS = (2, 4, 8, 16)
PAD = 16
RAW, SPLIT = 4, 2
STAGE0 = 7
CHUNK = 2
STAGE = 4
MC = 512


class Steps:

    def __init__(self, sem):
        self.sem, self.n, self.i, self.per = sem, 0, None, 0

    def done(self, instruction):
        self.n += 1
        instruction.then_inc(self.sem, 1)

    def wait(self, engine):
        engine.wait_ge(self.sem, self.n if self.i is None else self.i * self.per + self.n)

    def loop(self, i, per):
        self.i, self.per, self.first = i, per, self.n

    def end(self, turns):
        assert self.n - self.first == self.per, (self.n - self.first, self.per)
        self.n = self.first + self.per * turns
        self.i = None


def trunk_kernel(nc, x, c, ada_w, ada_b, norm_mix_g, w_in, b_in, conv_w, conv_b, lru_wa, lru_ba, lru_wx,
                 lru_bx, lru_lambda, pool_w, pool_b, pool_scale, proj_a, proj_b, w_out, norm_ffn_g, w_up,
                 ffn_conv_w, ffn_conv_b, w_down, final_g, out):
    S, D = x.shape[1], x.shape[2]
    NT = D // P
    ST = S // P
    NQ = NT // QT
    DF = w_down.shape[1]
    GROUPS = DF // P // QT
    HEADS = lru_wa.shape[1]
    TAPS = conv_w.shape[1]
    PAIRS = NT // 2
    PT = pool_b.shape[1] // P
    GT, XP, GA, GB = NT, 2 * NT, 2 * NT + PT, 3 * NT + PT
    assert (S, NT, NQ, HEADS, PAIRS, PT, TAPS) == (512, 16, 4, 8, 8, 8, 4) and lru_wa.shape[2] == UC

    U_P3 = NQ * 3
    U_GB0 = U_P3 + NQ
    U_PW = U_GB0 + NQ
    U_GB1 = U_PW + 2
    U_B = U_GB1 + NQ
    B_SEG = 6
    B_TURNS = 3
    EARLY = 2
    R_BLOCK = EARLY + 2 * B_TURNS
    U_B2 = U_B + 2 * B_SEG * B_TURNS
    U_R = U_B2 + 4
    R_SEG = 9
    R_HEADS = 4
    R_TURNS = HEADS // R_HEADS
    U_M = U_R + R_SEG * HEADS
    U_O = U_M + 8 * PAIRS
    U_F = U_O + 4 * PAIRS
    U_L = U_F + 16
    F_SEG = 24
    U_D = U_L + F_SEG * (GROUPS - 1)
    UNITS = U_D + 8
    LRU_LOADS = R_TURNS

    def rows(w):
        return w.rearrange("(t p) n -> p t n", p=P)

    win_v, wup_v, wdn_v, wout_v = rows(w_in[0]), rows(w_up[0]), rows(w_down[0]), rows(w_out[0])
    pa_v, pb_v, ada_v = rows(proj_a[0]), rows(proj_b[0]), rows(ada_w[0])
    pw_v = pool_w[0].rearrange("g (k p) n -> p (g k) n", p=P)
    wa_v = lru_wa[0].rearrange("h (k p) n -> p (h k) n", p=P)
    wx_v = lru_wx[0].rearrange("h (k p) n -> p (h k) n", p=P)
    x_v = x[0].rearrange("(s p) d -> p s d", p=P)
    out_v = out[0].rearrange("(s p) d -> p s d", p=P)
    resid_spill = nc.dram_tensor("resid_spill", (P, NT, S), F32, kind="Internal").ap()
    pool_spill = nc.dram_tensor("pool_spill", (P, NT, S), F32, kind="Internal").ap()

    def by_tile(v):
        return v.rearrange("a (t p) -> (a t) p", p=P)

    FT = 2 * DF // P
    packs = [[("c", c), ("g_mix", norm_mix_g), ("ada_b", ada_b)],
             [("b_in", b_in), ("conv_b", conv_b), ("ba", lru_ba), ("bx", lru_bx), ("pool_b", pool_b)],
             [("conv_w", conv_w[0]), ("lam", lru_lambda), ("pool_s", pool_scale), ("g_ffn", norm_ffn_g),
              ("g_out", final_g.rearrange("(a n) -> a n", a=1))],
             [("ffn_b", ffn_conv_b)],
             [("ffn_w0", ffn_conv_w[0][0:1])], [("ffn_w1", ffn_conv_w[0][1:2])], [("ffn_w2", ffn_conv_w[0][2:3])]]
    NP = len(packs)
    place, pack_rows, param_loads = {}, [], []
    for n, pack in enumerate(packs):
        at = 0
        for name, v in pack:
            count = v.shape[0] * v.shape[1] // P
            place[name] = n * P + at
            param_loads.append((n, at, count, by_tile(v)))
            at += count
        assert at <= P
        pack_rows.append(at)

    ctx = ExitStack()
    with ctx:
        def sem(name):
            return ctx.enter_context(nc.semaphore(name))

        base = -(-nc.sbuf_base // 64) * 64
        top = [0]

        def at(name, shape, dt, offset):
            size = 4
            for n in shape[1:]:
                size *= n
            top[0] = max(top[0], offset + size)
            return nc.alloc_sbuf_tensor_at(name, shape, dt, offset=base + offset)

        TILE = 4 * S
        PAIR = 2 * TILE
        A, B, B2, C = 0, 64 * KB, 96 * KB, 128 * KB
        col_hi = at("col_hi", [P, NT, S], F32R, A)
        col_lo = at("col_lo", [P, NT, S], F32R, A + 32 * KB)
        pack_in = at("pack_in", [P, NP, P], F32, A)
        square_out = at("square_out", [P, D], F32, A + 8 * KB)
        rows_out = at("rows_out", [P, ST, D], F32, A)
        br_hi = at("br_hi", [P, NT, S], F32R, B)
        br_lo = at("br_lo", [P, NT, S], F32R, B + 32 * KB)
        x_rows = at("x_rows", [P, ST, D], F32, B)
        xn = at("xn", [P, NT, S], F32, B)
        ada_stage0 = at("ada_stage0", [P, STAGE0, CHUNK, MC], F32, B2)
        ada_acc0 = at("ada_acc0", [P, 2, MC], F32, B2 + STAGE0 * 4 * KB)
        yb_hi = at("yb_hi", [P, PT, S], F32R, B)
        yb_lo = at("yb_lo", [P, PT, S], F32R, B + 16 * KB)
        pool_hi = at("pool_hi", [P, PT, S], F32R, B2)
        pool_lo = at("pool_lo", [P, PT, S], F32R, B2 + 16 * KB)
        resid = at("resid", [P, NT, S], F32, B)
        u_hi = at("u_hi", [P, QT, S], F32R, B2)
        u_lo = at("u_lo", [P, QT, S], F32R, B2 + 8 * KB)
        sq = at("sq", [P, 2, S], F32, B2 + 16 * KB)
        sq_sum = at("sq_sum", [P, S], F32, B2 + 20 * KB)
        h2f = at("h2f", [P, QT, S], F32, B2 + 22 * KB)
        xT = at("xT", [P, NT, S], F32, C)
        z = at("z", [P, 2, PAD + S], F32, C)
        Z1 = C + 8 * (PAD + S)
        win_a = at("win_a", [P, 2, PAD + S], F32, Z1)
        win_b = at("win_b", [P, 2, PAD + S], F32, Z1 + 8 * (PAD + S))
        Z2 = Z1 + 16 * (PAD + S)
        ybf = at("ybf", [P, 2, S], F32, Z2)
        gate_b = at("gate_b", [P, 2, 2, S], F32, Z2 + PAIR)
        pbf = at("pbf", [P, 2, S], F32, Z2 + 3 * PAIR)
        count_fix = at("count_fix", [P, len(WINDOWS), 2, PAD], F32, Z2 + 4 * PAIR)
        xr = at("xr", [P, 2, S], F32, Z1)
        xr_hi = at("xr_hi", [P, 2, S], F32R, Z1 + PAIR)
        xr_lo = at("xr_lo", [P, 2, S], F32R, Z1 + 2 * PAIR)
        decay = at("decay", [P, 2, S], F32, Z1 + 3 * PAIR)
        inp = at("inp", [P, 2, S], F32, Z1 + 4 * PAIR)
        tanh_q = at("tanh_q", [P, 2, S], F32, Z1 + 5 * PAIR)
        gelu = at("gelu", [P, 2, S], F32, Z1 + 6 * PAIR)
        merged = at("merged", [P, NT, S], F32, C)
        conv_a = at("conv_a", [P, 2, S], F32, C)
        conv_l = at("conv_l", [P, 2, S], F32, C + PAIR)
        silu_a = at("silu_a", [P, 2, 2, S], F32, C + 2 * PAIR)
        scaled = at("scaled", [P, 2, 2, S], F32, C + 4 * PAIR)
        W = Z1 + 7 * PAIR
        UNIT = 4 * QT * UC
        w_raw = at("w_raw", [P, RAW, QT, UC], F32, W)
        w_hi = at("w_hi", [P, SPLIT, QT, UC], F32R, W + RAW * UNIT)
        w_lo = at("w_lo", [P, SPLIT, QT, UC], F32R, W + (RAW + SPLIT) * UNIT)
        K = W + (RAW + 2 * SPLIT) * UNIT
        par = at("par", [P, NP * P], F32, K)
        mod = at("mod", [P, 6 * NT], F32, K + 4 * NP * P)
        K2 = K + 4 * NP * P + 24 * NT
        ident = at("ident", [P, P], F32, K2)
        ones = at("ones", [P, P], F32, K2 + 512)
        K3 = K2 + 1024
        names = ["cact", "gain1", "gain2", "lam_abs", "lam_neg", "sig_l", "ser_s", "ser_s2", "ser_p", "rate", "neg_rate"]
        small = {n: at(n, [P, NT], F32, K3 + 4 * NT * k) for k, n in enumerate(names)}
        row_sq = at("row_sq", [P, ST], F32, K3 + 4 * NT * len(names))
        row_rstd = at("row_rstd", [P, ST], F32, K3 + 4 * NT * len(names) + 32)
        K4 = K3 + 4 * NT * len(names) + 64
        ada_acc = at("ada_acc", [P, MC], F32, K4)
        rstd_bc = at("rstd_bc", [P, S], F32, K4)
        ada_stage = at("ada_stage", [P, STAGE, MC], F32, K4 + 4 * MC)
        rstd_wide = at("rstd_wide", [P, ST, P], F32, K4 + 4 * MC)
        ada_acc1 = at("ada_acc1", [P, 2, MC], F32, K4 + 8 * MC)
        gate_a = at("gate_a", [P, 2, S], F32, K4 + 4 * MC)
        pb_in = at("pb_in", [P, 2, S], F32, K4 + 4 * MC + PAIR)
        assert base + top[0] <= nc.sbuf_usable_end, (base + top[0], nc.sbuf_usable_end)

        ps = ctx.enter_context(nc.psum_tensor("ps", [P, 8, S], F32))

        def col(name, t, n=1):
            if isinstance(t, int):
                return par[:, place[name] + t:place[name] + t + n]
            return par[:, bass.ds(t + place[name], n)]

        def cols(tensor, t, n=1):
            return tensor[:, t:t + n] if isinstance(t, int) else tensor[:, bass.ds(t, n)]

        SH1, SC1, GT1, SH2, SC2, GT2 = (k * NT for k in range(6))

        w_loaded = [sem(f"w_loaded{k}") for k in range(RAW)]
        hi_made, lo_made, unit_done = sem("hi_made"), sem("lo_made"), sem("unit_done")
        pack0_in, params_in, x_in = sem("pack0_in"), sem("params_in"), [sem(f"x_in{s}") for s in range(ST)]
        ada0_in = [sem(f"ada0_in{k}") for k in range(STAGE0)]
        ada_in = [sem(f"ada_in{k}") for k in range(STAGE)]
        const_ready, pads_ready = sem("const_ready"), sem("pads_ready")
        par_turned, par_ready, sig_c, cact_ready = sem("par_turned"), sem("par_ready"), sem("sig_c"), sem("cact_ready")
        sq_rows, rstd_rows, rstd_cast, rstd_ready = sem("sq_rows"), sem("rstd_rows"), sem("rstd_cast"), sem("rstd_ready")
        std_rows, rstd_spread = sem("std_rows"), sem("rstd_spread")
        x_turned, xT_ready, xn_ready = sem("x_turned"), sem("xT_ready"), sem("xn_ready")
        mac0, shared0, reduced0, mod0_ready = sem("mac0"), sem("shared0"), sem("reduced0"), sem("mod0_ready")
        h_ready, h_hi, h_lo = sem("h_ready"), sem("h_hi"), sem("h_lo")
        spilled = sem("spilled")
        z_ready, pool_f, pool_hi_ready, pool_lo_ready = sem("z_ready"), sem("pool_f"), sem("pool_hi_ready"), sem("pool_lo_ready")
        yb_f, yb_hi_ready, yb_lo_ready = sem("yb_f"), sem("yb_hi_ready"), sem("yb_lo_ready")
        gate_ready, pb_made = sem("gate_ready"), sem("pb_made")
        mac, reduced, mod_ready = sem("mac"), sem("reduced"), sem("mod_ready")
        rate_in, lam_sig, rate_ready = sem("rate_in"), sem("lam_sig"), sem("rate_ready")
        r_ready, tanh_ready = sem("r_ready"), sem("tanh_ready")
        xr_ready, xr_hi_ready, xr_lo_ready = sem("xr_ready"), sem("xr_hi_ready"), sem("xr_lo_ready")
        gates_ready, decay_ready, decay_sq = sem("gates_ready"), sem("decay_ready"), sem("decay_sq")
        var_ready, root_ready, gelu_ready = sem("var_ready"), sem("root_ready"), sem("gelu_ready")
        ya_f, ya_hi_ready, ya_lo_ready = sem("ya_f"), sem("ya_hi_ready"), sem("ya_lo_ready")
        pb_back, merged_ready, mg_hi, mg_lo = sem("pb_back"), sem("merged_ready"), sem("mg_hi"), sem("mg_lo")
        resid_in = [sem(f"resid_in{q}") for q in range(NQ)]
        x2_ready, sq_ready, sq_used = sem("x2_ready"), sem("sq_ready"), sem("sq_used")
        sum2, var2, std2, xn2_ready, h2_ready = sem("sum2"), sem("var2"), sem("std2"), sem("xn2_ready"), sem("h2_ready")
        h2_hi, h2_lo = sem("h2_hi"), sem("h2_lo")
        tap_ready, conv_ready, silu_ready = sem("tap_ready"), sem("conv_ready"), sem("silu_ready")
        uf_ready, u_hi_ready, u_lo_ready, down_added = sem("uf_ready"), sem("u_hi_ready"), sem("u_lo_ready"), sem("down_added")
        scaled_ready, turned, rows_ready = sem("scaled_ready"), sem("turned"), sem("rows_ready")
        sum3, var3, std3, rstd3 = sem("sum3"), sem("var3"), sem("std3"), sem("rstd3")
        rows_act, rows_dve, out_stored = sem("rows_act"), sem("rows_dve"), sem("out_stored")
        steps_v = sem("steps_v")

        first_blocks = [b for q in range(NQ) for b in (SC1 // QT + q, SH1 // QT + q)]
        LATER = GT1 // QT
        CH = NT // CHUNK
        QC = 2 * CH
        SHARE = {b: () if b < 2 else ((0, 1), ())[b % 2] for b in range(2 * NQ)}

        def chunk_of(n):
            return n // CH, n % CH, n % CH in SHARE[n // CH]

        def summed(n):
            ours = sum(chunk_of(m)[2] for m in range(n + 1))
            return CHUNK * (n + 1 - ours), ours

        X_BEFORE = {1: 0, 2: 1, 3: 2, 4: 3}
        UNIT_BEFORE = {11: 0, 12: 1, 18: 2, 20: 3}
        SPLIT_FIRST = 13
        SPLIT_AFTER = (9, 13, 17)
        split_due = {QC * (q + 1) + k: 3 * q + 2 + r for q in range(NQ - 1) for r, k in enumerate(SPLIT_AFTER)}
        h_lo_due = {QC * (q + 1) + 1: q for q in range(NQ - 1)}
        B_FEED = (0, 1, 2, 3)
        R_FEED = (0, 1, 2, 5)
        R_SUM = (1, 2, 4, 6)

        DVE_ROWS, ACT_ROWS = (0, 1), (2, 3)
        OUT_PARTS = (slice(0, D // 2), slice(D // 2, D - UC))
        MERGE_AT = {4: (0, 1), 5: (2, 3), 6: (4, 5)}

        EARLY_FEED = ((U_P3, U_P3 + 1, U_P3 + 3, U_GB0 + 1), (U_GB0 + 3, U_PW + 1, U_GB1, U_GB1 + 1))
        EARLY_SUM = ((U_P3 + 1, U_P3 + 2, U_GB0, U_GB0 + 2), (U_PW, U_GB1, U_GB1 + 1, U_GB1 + 2))
        LRU_UNITS = [U_R + R_SEG * k + 6 for k in range(R_HEADS)]
        assert sorted(u % RAW for u in LRU_UNITS) == list(range(RAW))

        def lru_extra(u):
            return sum(k % RAW == u % RAW and k <= u for k in LRU_UNITS), 1

        def win_of(p):
            return (win_a, win_b)[p % 2]

        def span(start, n):
            return slice(start, start + n) if isinstance(start, int) else bass.ds(start, n)

        block = ctx.enter_context(nc.Block())

        @block.sync
        def _(sp):
            def load(u, src, i=None, n=0, dst=None):
                if i is not None:
                    sp.wait_ge(lo_made, i * n + (u - RAW + 1))
                elif u >= RAW:
                    sp.wait_ge(lo_made, u - RAW + 1)
                sp.dma_start(w_raw[:, u % RAW] if dst is None else dst, src).then_inc(w_loaded[u % RAW], 16)

            def at_reg(v):
                return v if isinstance(v, int) else sp.snap(v)

            def win(tile, q):
                return win_v[:, q * QT:(q + 1) * QT, span(at_reg(tile * P), UC)]

            def ada0(n):
                blk, k = first_blocks[n // CH], n % CH
                if n >= STAGE0:
                    rows_done, shares_done = summed(n - STAGE0)
                    if chunk_of(n - STAGE0)[2]:
                        sp.wait_ge(shared0, shares_done)
                    else:
                        sp.wait_ge(mac0, rows_done)
                sp.dma_start(ada_stage0[:, n % STAGE0], ada_v[:, k * CHUNK:(k + 1) * CHUNK, blk * MC:(blk + 1) * MC]
                             ).then_inc(ada0_in[n % STAGE0], 16)

            def p_unit(u):
                return win(XP + 2 * (u % 3), u // 3) if u < U_P3 else win(XP + 6, u - U_P3)

            for n, a, count, v in param_loads:
                if n == 0:
                    sp.dma_start(pack_in[a:a + count, n], v).then_inc(pack0_in, 16)
            for n in range(QC * NQ):
                if n in X_BEFORE:
                    s = X_BEFORE[n]
                    sp.dma_start(x_rows[:, s], x_v[:, s]).then_inc(x_in[s], 16)
                if n in UNIT_BEFORE:
                    load(UNIT_BEFORE[n], p_unit(UNIT_BEFORE[n]))
                ada0(n)
                if n - STAGE0 in (SPLIT_FIRST + 1, SPLIT_FIRST + 2):
                    u = n - STAGE0 - SPLIT_FIRST - 1 + RAW
                    load(u, p_unit(u))
                if n - STAGE0 in split_due:
                    u = split_due[n - STAGE0] + RAW
                    load(u, p_unit(u))
            u_next = max(v for c_, v in split_due.items() if c_ + STAGE0 < QC * NQ) + 1 + RAW
            load(u_next, p_unit(u_next))
            load(u_next + 1, p_unit(u_next + 1))
            sp.wait_ge(xT_ready, NT)
            for half in range(2):
                hs = slice(half * NT // 2, (half + 1) * NT // 2)
                sp.dma_start(resid_spill[:, hs], xT[:, hs]).then_inc(spilled, 16)
                if half == 0:
                    load(u_next + 2, p_unit(u_next + 2))
            for u in range(u_next + 3, U_GB0):
                load(u, p_unit(u))
            for q in range(NQ):
                load(U_GB0 + q, win(GB, q))
            for k in range(2):
                load(U_PW + k, pw_v[:, k * QT:(k + 1) * QT, :])
            for q in range(NQ):
                load(U_GB1 + q, win(GB + 2, q))

            def proj_b_unit(j, k):
                return pb_v[:, k * QT:(k + 1) * QT, span(at_reg(j * UC), UC)]

            with sp.Fori(0, B_TURNS) as i:
                for half in range(2):
                    for k in range(B_SEG):
                        j = i * 2 + half
                        load(U_B + half * B_SEG + k, proj_b_unit(j, k) if k < 2 else win(j * 2 + (GB + 4), k - 2),
                             i, 2 * B_SEG)
            for k in range(4):
                load(U_B2 + k, proj_b_unit(2 * B_TURNS + k // 2, k % 2))

            with sp.Fori(0, R_TURNS) as i:
                for head in range(R_HEADS):
                    for k in range(R_SEG):
                        u, n = U_R + head * R_SEG + k, R_SEG * R_HEADS
                        tile = i * (2 * R_HEADS) + 2 * head
                        if k == 6:
                            rows_of = bass.ds(sp.snap(tile), 2)
                            load(u, wa_v[:, rows_of, :], i, n, w_raw[:, u % RAW, 0:2])
                            sp.dma_start(w_raw[:, u % RAW, 2:4], wx_v[:, rows_of, :]).then_inc(w_loaded[u % RAW], 16)
                        else:
                            load(u, win(tile, k) if k < 4 else win(tile + GT, k - 4 if k < 6 else k - 5), i, n)

            with sp.Fori(0, PAIRS) as i:
                for k in range(8):
                    load(U_M + k, win(i * 2 + GA, k) if k < 4 else
                         pa_v[:, (k - 4) * QT:(k - 3) * QT, bass.ds(sp.snap(i * UC), UC)], i, 8)

            def out_unit(k, d):
                return wout_v[:, k * QT:(k + 1) * QT, span(at_reg(d * UC), UC)]

            for k in range(4):
                load(U_O + k, out_unit(k, 0))
            sp.wait_ge(unit_done, U_O)
            sp.wait_ge(spilled, 16 * (PAIRS + 2))
            for k in range(4):
                cs = slice(k * QT, (k + 1) * QT)
                sp.dma_start(resid[:, cs], resid_spill[:, cs]).then_inc(resid_in[k], 16)
                load(U_O + 4 + k, out_unit(k, 1))
            with sp.Fori(0, 3) as i:
                for half in range(2):
                    for k in range(4):
                        load(U_O + 8 + half * 4 + k, out_unit(k, i * 2 + (half + 2)), i, 8)

            def up(q, g, p):
                return wup_v[:, q * QT:(q + 1) * QT, span(at_reg(g * (QT * P) + ((p // 2) * UC + (p % 2) * DF)), UC)]

            def down(d, g):
                return wdn_v[:, span(at_reg(g * QT), QT), d * UC:(d + 1) * UC]

            for q in range(NQ):
                for p in range(4):
                    load(U_F + 4 * q + p, up(q, 0, p))
            with sp.Fori(0, GROUPS - 1) as i:
                for k in range(F_SEG):
                    load(U_L + k, up(k, i + 1, 0) if k < 4 else down(k - 4, i) if k < 12 else
                         up(k % 4, i + 1, (k - 8) // 4), i, F_SEG)
            for d in range(8):
                load(U_D + d, down(d, GROUPS - 1))
            for n in range(len(DVE_ROWS)):
                for half in range(2):
                    cs = slice(half * D // 2, (half + 1) * D // 2)
                    for rows_done, s in ((rows_dve, DVE_ROWS[n]), (rows_act, ACT_ROWS[n])):
                        sp.wait_ge(rows_done, 2 * n + half + 1)
                        sp.dma_start(out_v[:, s, cs], rows_out[:, s, cs]).then_inc(out_stored, 16)
            sp.wait_ge(out_stored, 16 * 2 * ST)

        @block.gpsimd
        def _(pool):
            pool.memset(ones[:], 1.0).then_inc(const_ready, 1)
            pool.memset(ident[:], 0.0).then_inc(const_ready, 1)
            pool.wait_ge(const_ready, 2)
            pool.affine_select(out=ident[:], in_=ident[:], compare_op=ALU.not_equal, fill=1.0, base=0,
                               pattern=[[-1, P]], channel_multiplier=1).then_inc(const_ready, 1)
            pool.wait_ge(xT_ready, NT)
            pool.wait_ge(rstd_ready, 1)
            for t in range(NT):
                pool.tensor_tensor(xn[:, t], xT[:, t], rstd_bc[:], ALU.mult).then_inc(xn_ready, 1)
            pool.wait_ge(spilled, 32)
            pool.wait_ge(xn_ready, NT)
            pool.memset(z[:, :, 0:PAD], 0.0)
            pool.memset(count_fix[:], 1.0).then_inc(pads_ready, 1)
            pool.wait_ge(pads_ready, 1)
            for g, win_ in enumerate(WINDOWS):
                for t in range(win_ - 1):
                    last = pool.memset(count_fix[:, g, :, t:t + 1], win_ / (t + 1.0))
            last.then_inc(pads_ready, 1)

        @block.tensor
        def _(pe):
            def products(u, outs, hi, lo, ks=range(QT), start=True, stop=True, slot_of=None, last=True, i=None, n=0,
                         wait=True, tile_ready=None, tile0=0):
                if wait:
                    pe.wait_ge(lo_made, u + 1 if i is None else i * n + (u + 1))
                s = u % SPLIT
                order = [(m, a) for m in range(len(outs)) for a in range(len(ks))]
                if tile_ready is not None:
                    order.sort(key=lambda ma: ma[1])
                for m, a in order:
                        o, k = outs[m], ks[a]
                        if tile_ready is not None and m == 0:
                            pe.wait_ge(tile_ready, tile0 + k + 1)
                        block_of = k if slot_of is None else slot_of[a]
                        wh = w_hi[:, s, block_of, m * P:(m + 1) * P]
                        wl = w_lo[:, s, block_of, m * P:(m + 1) * P]
                        pe.matmul(o, wh, hi(k), start=start and a == 0, stop=False)
                        pe.matmul(o, wh, lo(k), start=False, stop=False)
                        mm = pe.matmul(o, wl, hi(k), start=False, stop=stop and a == len(ks) - 1)
                if last:
                    mm.then_inc(unit_done, 1)

            def banks(b):
                return [ps[:, b], ps[:, b + 1]]

            def tiles(hi, lo, q):
                return (lambda k: hi[:, q * QT + k]), (lambda k: lo[:, q * QT + k])

            def over_model(u, b, hi, lo, i=None, n=0, nq=NQ, qs=None):
                for q in range(nq) if qs is None else qs:
                    products(u + q, banks(b), *tiles(hi, lo, q), start=q == 0, stop=q == nq - 1, i=i, n=n)

            def turn_packs(ns):
                for n in ns:
                    r = pack_rows[n]
                    mm = pe.transpose(ps[:, 4 + n // 4, (n % 4) * P:(n % 4) * P + r], pack_in[0:r, n], ident[0:r, 0:r])
                mm.then_inc(par_turned, 1)

            pe.wait_ge(const_ready, 3)
            pe.wait_ge(pack0_in, 16 * sum(n == 0 for n, a, count, v in param_loads))
            turn_packs(range(1))
            for s in range(ST):
                pe.wait_ge(x_in[s], 16)
                for q in range(NQ):
                    if s:
                        pe.wait_ge(xT_ready, NQ * (s - 1) + q + 1)
                    for t in range(QT * q, QT * (q + 1)):
                        mm = pe.transpose(ps[:, q, (t % QT) * P:(t % QT + 1) * P], x_rows[:, s, t * P:(t + 1) * P], ident[:])
                    mm.then_inc(x_turned, 1)

            def spread(bank):
                for s in range(ST):
                    mm = pe.matmul(ps[:, bank, s * P:(s + 1) * P], rstd_wide[:, s], ident[:], start=True, stop=True)
                mm.then_inc(rstd_spread, 1)

            def position_sums(pairs, bank, sem_):
                pe.wait_ge(sq_used, pairs)
                for s in range(ST):
                    mm = pe.matmul(ps[:, bank, s:s + 1], sq_sum[:, s * P:(s + 1) * P], ones[:, 0:1], start=True, stop=True)
                mm.then_inc(sem_, 1)

            def share0(b):
                for k in SHARE[b]:
                    n = b * CH + k
                    pe.wait_ge(ada0_in[n % STAGE0], 16 * (n // STAGE0 + 1))
                    if k == SHARE[b][0]:
                        pe.wait_ge(mod0_ready, b - 1)
                    for r in range(CHUNK):
                        t = k * CHUNK + r
                        for m in range(QT):
                            mm = pe.matmul(ps[:, 6 + b % 2, b * QT + m:b * QT + m + 1],
                                           ada_stage0[:, n % STAGE0, r, m * P:(m + 1) * P], small["cact"][:, t:t + 1],
                                           start=k == SHARE[b][0] and r == 0 and m == 0, stop=False)
                    mm.then_inc(shared0, 1)

            def reduce0(b):
                pe.wait_ge(mac0, summed(CH * (b + 1) - 1)[0])
                for m in range(QT):
                    for acc in (ada_acc0, ada_acc1):
                        mm = pe.matmul(ps[:, 6 + b % 2, b * QT + m:b * QT + m + 1], acc[:, b % 2, m * P:(m + 1) * P],
                                       ones[:, 0:1], start=not SHARE[b] and m == 0 and acc is ada_acc0,
                                       stop=m == QT - 1 and acc is ada_acc1)
                mm.then_inc(reduced0, 1)

            def reduce(seg, bank, i=None, segs=0):
                pe.wait_ge(mac, NT * (seg + 1) if i is None else i * (segs * NT) + NT * (seg + 1))
                for m in range(QT):
                    mm = pe.matmul(ps[:, bank, m:m + 1], ada_acc[:, m * P:(m + 1) * P], ones[:, 0:1], start=True, stop=True)
                mm.then_inc(reduced, 1)

            pe.wait_ge(rstd_cast, 1)
            spread(6)
            pe.wait_ge(par_ready, 1)
            pe.wait_ge(params_in, 16 * sum(n > 0 for n, a, count, v in param_loads))
            turn_packs(range(1, NP))
            pe.wait_ge(rstd_ready, 1)
            reduce0(0)
            reduce0(1)
            for q in range(NQ):
                if q < NQ - 1:
                    share0(2 * q + 2)
                for p in range(3):
                    products(3 * q + p, banks(2 * p), *tiles(col_hi, col_lo, q), start=q == 0, stop=q == NQ - 1,
                             tile_ready=h_lo if p == 0 else None, tile0=QT * q)
                    if q < NQ - 1 and p != 1:
                        if p == 2:
                            share0(2 * q + 3)
                        reduce0(2 * q + 2 + p // 2)
            pe.wait_ge(mod0_ready, 2 * NQ)
            over_model(U_P3, 6, col_hi, col_lo)
            over_model(U_GB0, 0, col_hi, col_lo)
            pe.wait_ge(z_ready, len(WINDOWS))
            reduce(0, 7)
            pe.wait_ge(pool_lo_ready, len(WINDOWS))
            for g, b in enumerate((2, 4, 6, 0)):
                if g == 2:
                    pe.wait_ge(mod_ready, 1)
                if g == 3:
                    pe.wait_ge(gate_ready, 1)
                products(U_PW + g // 2, banks(b), (lambda k, g=g: pool_hi[:, 2 * g + k]),
                         (lambda k, g=g: pool_lo[:, 2 * g + k]), ks=range(2), slot_of=[2 * (g % 2), 2 * (g % 2) + 1],
                         last=g % 2 == 1, wait=g % 2 == 0)
            pe.wait_ge(yb_f, 1)
            over_model(U_GB1, 2, col_hi, col_lo)
            pe.wait_ge(yb_f, 3)
            with pe.Fori(0, B_TURNS) as i:
                for half in range(2):
                    u = U_B + half * B_SEG
                    over_model(u, 4, yb_hi, yb_lo, i, 2 * B_SEG, nq=2, qs=(0,))
                    reduce(EARLY + half - 1, 7, i, 2)
                    over_model(u, 4, yb_hi, yb_lo, i, 2 * B_SEG, nq=2, qs=(1,))
                    over_model(u + 2, 0, col_hi, col_lo, i, 2 * B_SEG)
            for j in range(2):
                over_model(U_B2 + 2 * j, (4, 2)[j], yb_hi, yb_lo, nq=2)
            with pe.Fori(0, R_TURNS) as i:
                n = R_SEG * R_HEADS
                for head in range(R_HEADS):
                    u, seg = U_R + head * R_SEG, R_BLOCK + head
                    over_model(u, 0, col_hi, col_lo, i, n, qs=(0,))
                    reduce(seg - 1, 4, i, R_HEADS)
                    over_model(u, 0, col_hi, col_lo, i, n, qs=(1, 2, 3))
                    over_model(u + 4, 2, col_hi, col_lo, i, n, qs=(0, 1))
                    for t in range(2):
                        pe.wait_ge(xr_lo_ready, i * (2 * R_HEADS) + (2 * head + t + 1))
                        for gate in range(2):
                            products(u + 6, banks(4 + 2 * gate), lambda k: xr_hi[:, k], lambda k: xr_lo[:, k], ks=[t],
                                     slot_of=[2 * gate + t], start=t == 0, stop=t == 1, last=t == gate == 1,
                                     wait=t == gate == 0, i=i, n=n)
                    over_model(u + 5, 2, col_hi, col_lo, i, n, qs=(2, 3))
            pe.wait_ge(gates_ready, HEADS)
            reduce(R_BLOCK + HEADS - 1, 4)
            with pe.Fori(0, PAIRS) as i:
                over_model(U_M, 0, col_hi, col_lo, i, 8)
                over_model(U_M + 4, 2, br_hi, br_lo, i, 8)
            for q in range(NQ):
                pe.wait_ge(mg_lo, 2 * (q + 1))
                over_model(U_O, 0, col_hi, col_lo, qs=(q,))
            over_model(U_O + 4, 2, col_hi, col_lo)
            with pe.Fori(0, 3) as i:
                over_model(U_O + 8, 0, col_hi, col_lo, i, 8)
                over_model(U_O + 12, 2, col_hi, col_lo, i, 8)
            position_sums(PAIRS, 4, sum2)
            pe.wait_ge(rstd_cast, 2)
            spread(5)
            for q in range(NQ):
                for p in range(4):
                    if q == 0 and p == 0:
                        products(U_F, banks(0), *tiles(col_hi, col_lo, 0), stop=False, tile_ready=h2_lo)
                        continue
                    if p == 0:
                        pe.wait_ge(h2_lo, QT * (q + 1))
                    products(U_F + 4 * q + p, banks(2 * p), *tiles(col_hi, col_lo, q), start=q == 0, stop=q == NQ - 1)

            def down(u, d, i=None):
                if d >= 2:
                    base_ = 0 if i is not None else 8 * (GROUPS - 1)
                    pe.wait_ge(down_added, base_ + d - 1 if i is None else i * 8 + (d - 1))
                products(u + d, banks(4 + 2 * (d % 2)), lambda k: u_hi[:, k], lambda k: u_lo[:, k], i=i, n=F_SEG)

            with pe.Fori(0, GROUPS - 1) as i:
                over_model(U_L, 0, col_hi, col_lo, i, F_SEG)
                pe.wait_ge(u_lo_ready, i * 2 + 2)
                for d in range(8):
                    down(U_L + 4, d, i)
                over_model(U_L + 12, 2, col_hi, col_lo, i, F_SEG)
                over_model(U_L + 16, 4, col_hi, col_lo, i, F_SEG)
                over_model(U_L + 20, 6, col_hi, col_lo, i, F_SEG)

            def turn(d):
                pe.wait_ge(scaled_ready, d + 1)
                if d >= 2:
                    pe.wait_ge(rows_ready, d - 1)
                for s in range(ST):
                    for m in range(2):
                        o = ps[:, 2 * (d % 2) + s // 2, (s % 2) * UC + m * P:(s % 2) * UC + (m + 1) * P]
                        mm = pe.transpose(o, scaled[:, d % 2, m, s * P:(s + 1) * P], ident[:])
                mm.then_inc(turned, 1)

            for half in range(2):
                pe.wait_ge(u_lo_ready, 2 * GROUPS - 1 + half)
                for d in range(2):
                    products(U_D + d, banks((4, 2)[d]), lambda k: u_hi[:, k], lambda k: u_lo[:, k],
                             ks=range(2 * half, 2 * half + 2), start=half == 0, stop=half == 1, last=half == 1)
            for d in range(2, 8):
                down(U_D, d)
                turn(d - 2)
            turn(6)
            position_sums(2 * PAIRS, 4, sum3)
            turn(7)

        @block.scalar
        def _(act):
            def split(u, i=None, n=0, extra=0, extra_n=0):
                need = 16 * (u // RAW + 1 + extra)
                act.wait_ge(w_loaded[u % RAW], need if i is None else i * (16 * (n // RAW + extra_n)) + need)
                if u >= SPLIT:
                    act.wait_ge(unit_done, u - 1 if i is None else i * n + (u - 1))
                act.activation(w_hi[:, u % SPLIT], w_raw[:, u % RAW], ACT.Copy).then_inc(hi_made, 1)

            def split_range(us, extra=0):
                for u in us:
                    split(u, extra=extra)

            def feed(seg, quarter, i=None, segs=0):
                for t in range(STAGE * quarter, STAGE * (quarter + 1)):
                    start = (LATER + seg) * MC if i is None else act.snap(i * (segs * MC) + (LATER + seg) * MC)
                    if seg or quarter:
                        done = NT * seg + t - STAGE + 1
                        act.wait_ge(mac, done if i is None else i * (segs * NT) + done)
                    act.dma_start(ada_stage[:, t % STAGE], ada_v[:, t, span(start, MC)]).then_inc(ada_in[t % STAGE], 16)

            def biased(outs, b, func, name, tile, sem_, count=2):
                for m in range(count):
                    a_ = act.activation(outs[m], ps[:, b + m], func, bias=col(name, tile + m), scale=1.0)
                a_.then_inc(sem_, 1)

            for n, a, count, v in param_loads:
                if n:
                    act.dma_start(pack_in[a:a + count, n], v).then_inc(params_in, 16)
            act.wait_ge(par_ready, 1)
            act.activation(small["cact"][:], col("c", 0, NT), ACT.Sigmoid).then_inc(sig_c, 1)
            for s in range(ST):
                act.wait_ge(x_in[s], 16)
                if s:
                    act.wait_ge(sq_rows, s)
                act.activation(square_out[:], x_rows[:, s], ACT.Square, accum_out=row_sq[:, s:s + 1]).then_inc(sq_rows, 1)
                for q in range(NQ):
                    act.wait_ge(x_turned, NQ * s + q + 1)
                    act.activation(xT[:, QT * q:QT * (q + 1), s * P:(s + 1) * P],
                                   ps[:, q].rearrange("p (t c) -> p t c", t=QT), ACT.Copy).then_inc(xT_ready, 1)
            act.wait_ge(rstd_rows, 1)
            act.activation(row_rstd[:], row_rstd[:], ACT.Sqrt).then_inc(std_rows, 1)
            split(0)
            split(1)

            def h_quarter(q):
                act.wait_ge(mod0_ready, 2 * (q + 1))
                act.wait_ge(xn_ready, QT * (q + 1))
                def high(t):
                    act.wait_ge(h_ready, t + 1)
                    act.activation(col_hi[:, t], xn[:, t], ACT.Copy).then_inc(h_hi, 1)

                for t in range(QT * q, QT * (q + 1)):
                    act.activation(xn[:, t], xn[:, t], ACT.Identity, bias=mod[:, SH1 + t:SH1 + t + 1],
                                   scale=small["gain1"][:, t:t + 1]).then_inc(h_ready, 1)
                    if t > QT * q:
                        high(t - 1)
                high(QT * (q + 1) - 1)

            for q in range(NQ):
                h_quarter(q)
                if q < NQ - 1:
                    split_range(range(3 * q + 2, 3 * q + 5))

            def pool_in(p, b):
                if p == 0:
                    act.wait_ge(pads_ready, 2)
                else:
                    act.wait_ge(pool_f, p)
                biased([z[:, m, PAD:] for m in range(2)], b, ACT.Identity, "b_in", XP + 2 * p, z_ready)
                if p == len(WINDOWS) - 1:
                    split(U_GB0 + 2)
                act.wait_ge(pool_f, p + 1)
                act.activation(pool_hi[:, 2 * p:2 * p + 2], win_of(p)[:, :, PAD:], ACT.Copy).then_inc(pool_hi_ready, 1)

            for p in range(3):
                split(9 + p + 2)
                pool_in(p, 2 * p)
            def position(u):
                if u != U_GB0:
                    split(u + 2)
                for seg in range(EARLY):
                    if u in EARLY_FEED[seg]:
                        feed(seg, EARLY_FEED[seg].index(u))

            for u in range(U_P3, U_GB0):
                position(u)
            pool_in(3, 6)
            for u in range(U_GB0, U_PW):
                position(u)
            act.wait_ge(rate_in, 1)
            act.activation(small["sig_l"][:], small["lam_abs"][:], ACT.Sigmoid, scale=-1.0).then_inc(lam_sig, 1)
            biased([gate_b[:, 0, m] for m in range(2)], 0, ACT.Sigmoid, "b_in", GB, gate_ready)
            for k in range(2):
                position(U_PW + k)
                for g in (2 * k, 2 * k + 1):
                    act.wait_ge(yb_f, g + 1)
                    act.activation(yb_hi[:, 2 * g:2 * g + 2], ybf[:], ACT.Copy).then_inc(yb_hi_ready, 1)
            for u in range(U_GB1, U_B):
                position(u)
            biased([gate_b[:, 1, m] for m in range(2)], 2, ACT.Sigmoid, "b_in", GB + 2, gate_ready)

            def store_pb(j, i=None):
                start = 2 * j if i is None else act.snap(i * 4 + 2 * j)
                act.wait_ge(pb_made, j + 1 if i is None else i * 2 + (j + 1))
                act.dma_start(pool_spill[:, span(start, 2)], pbf[:]).then_inc(spilled, 16)

            with act.Fori(0, B_TURNS) as i:
                for half in range(2):
                    for k in range(B_SEG):
                        split(U_B + half * B_SEG + k + 2, i, 2 * B_SEG)
                        if k == 2:
                            store_pb(half, i)
                        if k in B_FEED:
                            feed(EARLY + half, B_FEED.index(k), i, 2)
                        if k == 5:
                            biased([gate_b[:, half, m] for m in range(2)], 0, ACT.Sigmoid, "b_in",
                                   i * 4 + (2 * half + GB + 4), gate_ready)
            for k in range(4):
                split(U_B2 + k + 2)
                if k % 2:
                    store_pb(2 * B_TURNS + k // 2)

            with act.Fori(0, R_TURNS) as i:
                n = R_SEG * R_HEADS
                for head in range(R_HEADS):
                    seg, tile = R_BLOCK + head, i * (2 * R_HEADS) + 2 * head
                    nth = i * R_HEADS + (head + 1)
                    for k in range(R_SEG):
                        u = U_R + head * R_SEG + k + 2
                        split(u, i, n, *lru_extra(u))
                        if k == 4:
                            for m in range(2):
                                act.wait_ge(xr_ready, i * (2 * R_HEADS) + (2 * head + m + 1))
                                act.activation(xr_hi[:, m], xr[:, m], ACT.Copy).then_inc(xr_hi_ready, 1)
                        if k in R_FEED:
                            feed(seg, R_FEED.index(k), i, R_HEADS)
                        if k == 3:
                            biased([z[:, m, PAD:] for m in range(2)], 0, ACT.Identity, "b_in", tile, z_ready)
                        if k == 6:
                            biased([decay[:, m] for m in range(2)], 4, ACT.Sigmoid, "ba", tile, r_ready)
                            biased([inp[:, m] for m in range(2)], 6, ACT.Sigmoid, "bx", tile, gates_ready)
                            act.wait_ge(gates_ready, nth)
                            for m in range(2):
                                a_ = act.activation(tanh_q[:, m], decay[:, m], ACT.Tanh, scale=cols(small["rate"], tile + m))
                            a_.then_inc(tanh_ready, 1)
                        if k == 7:
                            act.wait_ge(tanh_ready, nth)
                            for m in range(2):
                                a_ = act.activation(decay[:, m], decay[:, m], ACT.Exp, scale=cols(small["neg_rate"], tile + m))
                            a_.then_inc(decay_ready, 1)
                            act.wait_ge(decay_ready, nth)
                            act.activation(z[:, :, PAD:], decay[:], ACT.Square).then_inc(decay_sq, 1)
                        if k == 8:
                            act.wait_ge(var_ready, nth)
                            act.activation(tanh_q[:], tanh_q[:], ACT.Sqrt).then_inc(root_ready, 1)
                            biased([gelu[:, m] for m in range(2)], 2, ACT.Gelu_apprx_tanh, "b_in", tile + GT, gelu_ready)
                            act.wait_ge(ya_f, nth)
                            act.activation(br_hi[:, bass.ds(act.snap(tile), 2)], gelu[:], ACT.Copy).then_inc(ya_hi_ready, 1)

            def merge_hi(d):
                act.wait_ge(merged_ready, d + 1)
                act.activation(col_hi[:, 2 * d:2 * d + 2], merged[:, 2 * d:2 * d + 2], ACT.Copy).then_inc(mg_hi, 1)

            def merge_position(k, i):
                split(U_M + k + 2, i, 8, LRU_LOADS)
                if k == 2:
                    pair = 2 * i if isinstance(i, int) else act.snap(i * 2)
                    act.dma_start(pb_in[:], pool_spill[:, span(pair, 2)]).then_inc(pb_back, 16)
                if k == 3:
                    biased([gate_a[:, m] for m in range(2)], 0, ACT.Sigmoid, "b_in", i * 2 + GA, gate_ready)

            with act.Fori(0, PAIRS - 1) as i:
                for k in range(8):
                    merge_position(k, i)
            for k in range(8):
                merge_position(k, PAIRS - 1)
                for d in MERGE_AT.get(k, ()):
                    merge_hi(d)

            def squares(d, i=None):
                start = 2 * d if i is None else act.snap(i * 4 + 2 * d)
                act.wait_ge(x2_ready, d + 1 if i is None else i * 2 + (d + 1))
                act.activation(sq[:], resid[:, span(start, 2)], ACT.Square).then_inc(sq_ready, 1)

            merge_hi(PAIRS - 2)
            for k in range(8):
                split(U_O + k + 2, extra=LRU_LOADS)
                if k == 0:
                    merge_hi(PAIRS - 1)
                if k % 4 == 3:
                    squares(k // 4)
            with act.Fori(0, 3) as i:
                for half in range(2):
                    for k in range(4):
                        split(U_O + 8 + half * 4 + k + 2, i, 8, LRU_LOADS)
                        if k == 3:
                            squares(half + 2, i)
            act.wait_ge(var2, 1)
            act.activation(row_rstd[:], row_rstd[:], ACT.Sqrt).then_inc(std2, 1)

            def h2_tile(t):
                act.wait_ge(xn2_ready, t + 1)
                act.activation(h2f[:, t % QT], h2f[:, t % QT], ACT.Identity, bias=mod[:, SH2 + t:SH2 + t + 1],
                               scale=small["gain2"][:, t:t + 1]).then_inc(h2_ready, 1)
                act.wait_ge(h2_ready, t + 1)
                act.activation(col_hi[:, t], h2f[:, t % QT], ACT.Copy).then_inc(h2_hi, 1)

            def conv_post(pair, b, nth, i, g4):
                buf = conv_l if pair % 2 else conv_a
                if pair >= 2:
                    act.wait_ge(u_lo_ready if pair % 2 else silu_ready, 1 if i is None else i * 2 + 3)
                for m in range(2):
                    tile = (2 * (pair // 2) + m + (pair % 2) * (DF // P)) + g4
                    a_ = act.activation(buf[:, m], ps[:, b + m], ACT.Identity, bias=col("ffn_b", tile), scale=col("ffn_w2", tile))
                a_.then_inc(tap_ready, 1)
                act.wait_ge(conv_ready, nth)
                if pair % 2 == 0:
                    act.activation(silu_a[:, pair // 2], conv_a[:], ACT.Silu).then_inc(silu_ready, 1)

            def u_high(pair, nth):
                act.wait_ge(uf_ready, nth)
                k = pair // 2
                act.activation(u_hi[:, 2 * k:2 * k + 2], conv_l[:], ACT.Copy).then_inc(u_hi_ready, 1)

            for t in range(QT):
                h2_tile(t)
            for k in range(16):
                if k + QT < NT:
                    h2_tile(k + QT)
                split(U_F + k + 2, extra=LRU_LOADS)
                if k >= 12:
                    pair = k - 12
                    conv_post(pair, 2 * pair, pair + 1, None, 0)
                    if pair % 2:
                        u_high(pair, pair // 2 + 1)
            with act.Fori(0, GROUPS - 1) as i:
                for k in range(F_SEG):
                    split(U_L + k + 2, i, F_SEG, LRU_LOADS)
                    if k in (3, 15, 19, 23):
                        pair = (3, 15, 19, 23).index(k)
                        conv_post(pair, 2 * pair, i * 4 + (5 + pair), i, i * QT + QT)
                        if pair % 2:
                            u_high(pair, i * 2 + (3 + pair // 2))

            def copy_rows(d):
                act.wait_ge(turned, d + 1)
                src = ps[:, 2 * (d % 2):2 * (d % 2) + 2].rearrange("p b (s c) -> p (b s) c", s=2)
                act.activation(rows_out[:, :, d * UC:(d + 1) * UC], src, ACT.Copy).then_inc(rows_ready, 1)

            for d in range(8):
                if U_D + d + 2 < UNITS:
                    split(U_D + d + 2, extra=LRU_LOADS)
                act.wait_ge(down_added, 8 * (GROUPS - 1) + d + 1)
                act.activation(sq[:], resid[:, 2 * d:2 * d + 2], ACT.Square).then_inc(sq_ready, 1)
                if d >= 2:
                    act.wait_ge(turned, d - 1)
                for m in range(2):
                    t = 2 * d + m
                    a_ = act.activation(scaled[:, d % 2, m], resid[:, t], ACT.Copy, scale=col("g_out", t))
                a_.then_inc(scaled_ready, 1)
                if d >= 2:
                    copy_rows(d - 2)
            copy_rows(6)
            act.wait_ge(var3, 1)
            act.activation(row_rstd[:], row_rstd[:], ACT.Sqrt).then_inc(std3, 1)
            act.wait_ge(rstd3, 1)
            for s in ACT_ROWS:
                for half, cs in enumerate(OUT_PARTS):
                    a_ = act.activation(rows_out[:, s, cs], rows_out[:, s, cs], ACT.Copy, scale=row_rstd[:, s:s + 1])
                    if half:
                        act.wait_ge(turned, PAIRS)
                        a_ = act.activation(rows_out[:, s, D - UC:], ps[:, 3, (s % 2) * UC:(s % 2 + 1) * UC], ACT.Copy,
                                            scale=row_rstd[:, s:s + 1])
                    a_.then_inc(rows_act, 1)

        @block.vector
        def _(v):
            own = Steps(steps_v)

            def split(u, i=None, n=0):
                v.wait_ge(hi_made, u + 1 if i is None else i * n + (u + 1))
                v.tensor_tensor(w_lo[:, u % SPLIT], w_raw[:, u % RAW], w_hi[:, u % SPLIT].bitcast(F32), ALU.subtract
                                ).then_inc(lo_made, 1)

            def low(out_, full, high, sem_):
                v.tensor_tensor(out_, full, high.bitcast(F32), ALU.subtract).then_inc(sem_, 1)

            def take_packs(ns, turn):
                v.wait_ge(par_turned, turn)
                for n in ns:
                    last = v.tensor_copy(par[:, n * P:n * P + pack_rows[n]], ps[:, 4 + n // 4, (n % 4) * P:(n % 4) * P + pack_rows[n]])
                last.then_inc(par_ready, 1)

            take_packs(range(1), 1)
            v.wait_ge(par_ready, 1)
            v.wait_ge(sig_c, 1)
            v.wait_ge(const_ready, 3)
            cact = small["cact"]
            v.tensor_tensor(cact[:], cact[:], col("c", 0, NT), ALU.mult).then_inc(cact_ready, 1)
            v.wait_ge(cact_ready, 1)

            def mac_chunk0(n):
                b, k, shared = chunk_of(n)
                if shared:
                    return
                so_far = summed(n)[0] - CHUNK
                v.wait_ge(ada0_in[n % STAGE0], 16 * (n // STAGE0 + 1))
                first = min(set(range(CH)) - set(SHARE[b]))
                if k == first and b >= 2:
                    v.wait_ge(reduced0, b - 1)
                for r in range(CHUNK):
                    t = k * CHUNK + r
                    w, acc = ada_stage0[:, n % STAGE0, r], (ada_acc0, ada_acc1)[r][:, b % 2]
                    if k == first:
                        v.tensor_scalar(acc, w, cact[:, t:t + 1], None, ALU.mult).then_inc(mac0, 1)
                    else:
                        v.wait_ge(mac0, so_far + r - 1)
                        v.scalar_tensor_tensor(acc, w, cact[:, t:t + 1], acc, ALU.mult, ALU.add).then_inc(mac0, 1)

            def mod0(b):
                v.wait_ge(reduced0, b + 1)
                t = first_blocks[b] * QT
                if b % 2 == 0:
                    own.done(v.tensor_tensor(mod[:, t:t + QT], ps[:, 6 + b % 2, b * QT:(b + 1) * QT], col("ada_b", t, QT), ALU.add))
                    own.wait(v)
                    k = t - SC1
                    v.scalar_tensor_tensor(small["gain1"][:, k:k + QT], mod[:, t:t + QT], 1.0, col("g_mix", k, QT),
                                           ALU.add, ALU.mult).then_inc(mod0_ready, 1)
                else:
                    v.tensor_tensor(mod[:, t:t + QT], ps[:, 6 + b % 2, b * QT:(b + 1) * QT], col("ada_b", t, QT), ALU.add
                                    ).then_inc(mod0_ready, 1)

            def widen_rstd():
                own.done(v.reciprocal(row_rstd[:], row_rstd[:]))
                own.wait(v)
                for s in range(ST):
                    last = v.tensor_scalar(rstd_wide[:, s], ones[:], row_rstd[:, s:s + 1], None, ALU.mult)
                last.then_inc(rstd_cast, 1)

            def h_low(q):
                for t in range(QT * q, QT * (q + 1)):
                    v.wait_ge(h_hi, t + 1)
                    low(col_lo[:, t], xn[:, t], col_hi[:, t], h_lo)

            for n in range(QC * NQ):
                mac_chunk0(n)
                if n == 10:
                    take_packs(range(1, NP), 2)
                if n == 5:
                    v.wait_ge(sq_rows, ST)
                    v.tensor_scalar(row_rstd[:], row_sq[:], 1.0 / D, EPS, ALU.mult, ALU.add).then_inc(rstd_rows, 1)
                if n == 6:
                    v.wait_ge(std_rows, 1)
                    widen_rstd()
                if n == 8:
                    v.wait_ge(rstd_spread, 1)
                    v.tensor_copy(rstd_bc[:], ps[:, 6]).then_inc(rstd_ready, 1)
                if n == SPLIT_FIRST:
                    split(0)
                    split(1)
                if n % CH == 2 and n > CH and n // CH % 2:
                    mod0(n // CH - 1)
                if n % QC == 0 and n:
                    mod0(n // CH - 1)
                if n in h_lo_due:
                    h_low(h_lo_due[n])
                if n in split_due:
                    split(split_due[n])
            mod0(2 * NQ - 1)
            for n in sorted(split_due):
                if n >= QC * NQ:
                    split(split_due[n])
            h_low(NQ - 1)

            def pool_windows(p):
                v.wait_ge(z_ready, p + 1)
                if p:
                    v.wait_ge(pool_lo_ready, p)
                src, step, bufs = z, 1, (win_a, win_b)
                for r in range(p + 1):
                    dst = bufs[r % 2]
                    lo_ = 2 * step - 1
                    own.done(v.tensor_tensor(dst[:, :, lo_:], src[:, :, lo_:], src[:, :, lo_ - step:PAD + S - step], ALU.add))
                    if r == 1 and p == len(WINDOWS) - 1:
                        split(U_GB0 + 2)
                    own.wait(v)
                    src, step = dst, 2 * step
                own.done(v.tensor_tensor(src[:, :, PAD:2 * PAD], src[:, :, PAD:2 * PAD], count_fix[:, p], ALU.mult))
                own.wait(v)
                assert src is win_of(p)
                v.scalar_tensor_tensor(src[:, :, PAD:], src[:, :, PAD:], 1.0 / WINDOWS[p], z[:, :, PAD:], ALU.mult,
                                       ALU.subtract).then_inc(pool_f, 1)
                v.wait_ge(pool_hi_ready, p + 1)
                low(pool_lo[:, 2 * p:2 * p + 2], src[:, :, PAD:], pool_hi[:, 2 * p:2 * p + 2], pool_lo_ready)

            def macs(seg, quarter, i=None, segs=0):
                for t in range(STAGE * quarter, STAGE * (quarter + 1)):
                    need = 16 * (NT // STAGE * seg + quarter + 1)
                    v.wait_ge(ada_in[t % STAGE], need if i is None else i * (16 * (NT // STAGE) * segs) + need)
                    w = ada_stage[:, t % STAGE]
                    if t == 0:
                        v.tensor_scalar(ada_acc[:], w, cact[:, 0:1], None, ALU.mult).then_inc(mac, 1)
                    else:
                        so_far = NT * seg + t
                        v.wait_ge(mac, so_far if i is None else i * (segs * NT) + so_far)
                        v.scalar_tensor_tensor(ada_acc[:], w, cact[:, t:t + 1], ada_acc[:], ALU.mult, ALU.add
                                               ).then_inc(mac, 1)

            def modulation(seg, bank, i=None, segs=0):
                t = (LATER + seg) * QT if i is None else v.snap(i * (segs * QT) + (LATER + seg) * QT)
                tb = (LATER + seg) * QT if i is None else i * (segs * QT) + (LATER + seg) * QT
                v.wait_ge(reduced, seg + 1 if i is None else i * segs + (seg + 1))
                v.tensor_tensor(mod[:, span(t, QT)], ps[:, bank, 0:QT], col("ada_b", tb, QT), ALU.add).then_inc(mod_ready, 1)

            def position(u):
                if u != U_GB0:
                    split(u + 2)
                if u == U_GB0 + 3:
                    modulation(0, 7)
                for seg in range(EARLY):
                    if u in EARLY_SUM[seg]:
                        macs(seg, EARLY_SUM[seg].index(u))

            for p in range(3):
                split(9 + p + 2)
                pool_windows(p)
            for u in range(U_P3, U_GB0):
                position(u)
            pool_windows(3)
            sm = small

            def step_(ins):
                own.done(ins)
                own.wait(v)

            step_(v.tensor_scalar(sm["lam_neg"][:], col("lam", 0, NT), -1.0, None, ALU.mult))
            v.tensor_tensor(sm["lam_abs"][:], sm["lam_neg"][:], col("lam", 0, NT), ALU.max).then_inc(rate_in, 1)
            for u in range(U_GB0, U_PW):
                position(u)
            v.wait_ge(lam_sig, 1)
            step_(v.tensor_scalar(sm["ser_p"][:], sm["sig_l"][:], -1.0, 2.0, ALU.mult, ALU.add))
            step_(v.reciprocal(sm["ser_s"][:], sm["ser_p"][:]))
            step_(v.tensor_tensor(sm["ser_s"][:], sm["ser_s"][:], sm["sig_l"][:], ALU.mult))
            step_(v.tensor_tensor(sm["ser_s2"][:], sm["ser_s"][:], sm["ser_s"][:], ALU.mult))
            step_(v.tensor_scalar(sm["ser_p"][:], sm["ser_s2"][:], 1.0 / 17, None, ALU.mult))
            for odd in (15, 13, 11, 9, 7, 5, 3):
                step_(v.scalar_tensor_tensor(sm["ser_p"][:], sm["ser_p"][:], 1.0 / odd, sm["ser_s2"][:], ALU.add, ALU.mult))
            step_(v.scalar_tensor_tensor(sm["ser_p"][:], sm["ser_p"][:], 1.0, sm["ser_s"][:], ALU.add, ALU.mult))
            step_(v.tensor_scalar(sm["lam_neg"][:], sm["lam_neg"][:], 0.0, None, ALU.max))
            step_(v.scalar_tensor_tensor(sm["rate"][:], sm["ser_p"][:], 2.0, sm["lam_neg"][:], ALU.mult, ALU.add))
            step_(v.tensor_scalar(sm["neg_rate"][:], sm["rate"][:], -LRU_C, None, ALU.mult))
            v.tensor_scalar(sm["rate"][:], sm["rate"][:], LRU_C, None, ALU.mult).then_inc(rate_ready, 1)

            for k in range(2):
                position(U_PW + k)
                for g in (2 * k, 2 * k + 1):
                    if g:
                        v.wait_ge(yb_lo_ready, g)
                    for m in range(2):
                        last = v.tensor_scalar(ybf[:, m], ps[:, (2, 4, 6, 0)[g] + m], col("pool_b", 2 * g + m),
                                               col("pool_s", 2 * g + m), ALU.add, ALU.mult)
                    last.then_inc(yb_f, 1)
                    v.wait_ge(yb_hi_ready, g + 1)
                    low(yb_lo[:, 2 * g:2 * g + 2], ybf[:], yb_hi[:, 2 * g:2 * g + 2], yb_lo_ready)
            for u in range(U_GB1, U_B):
                position(u)

            def share_b(j, i=None, b=4):
                v.wait_ge(gate_ready, j + 1 if i is None else i * 2 + (j + 1))
                v.wait_ge(spilled, 16 * (j + 2) if i is None else i * 32 + 16 * (j + 2))
                v.tensor_tensor(pbf[:], ps[:, b:b + 2], gate_b[:, j % 2], ALU.mult).then_inc(pb_made, 1)

            with v.Fori(0, B_TURNS) as i:
                for half in range(2):
                    for k in range(B_SEG):
                        split(U_B + half * B_SEG + k + 2, i, 2 * B_SEG)
                        if k == 1:
                            share_b(half, i)
                            modulation(EARLY + half - 1, 7, i, 2)
                        if k - 1 in B_FEED:
                            macs(EARLY + half, B_FEED.index(k - 1), i, 2)
            for k in range(4):
                split(U_B2 + k + 2)
                if k % 2:
                    share_b(2 * B_TURNS + k // 2, b=(4, 2)[k // 2])

            with v.Fori(0, R_TURNS) as i:
                n = R_SEG * R_HEADS
                own.loop(i, R_HEADS * (TAPS - 1 + 3))
                for head in range(R_HEADS):
                    seg, tile = R_BLOCK + head, i * (2 * R_HEADS) + 2 * head
                    nth = i * R_HEADS + (head + 1)
                    for k in range(R_SEG):
                        if k != 4:
                            split(U_R + head * R_SEG + k + 2, i, n)
                        if k == 1:
                            modulation(seg - 1, 4, i, R_HEADS)
                        if k == 4:
                            for m in range(2):
                                v.wait_ge(xr_hi_ready, i * (2 * R_HEADS) + (2 * head + m + 1))
                                low(xr_lo[:, m], xr[:, m], xr_hi[:, m], xr_lo_ready)
                        if k in R_SUM[:3]:
                            macs(seg, R_SUM.index(k), i, R_HEADS)
                        if k == 3:
                            v.wait_ge(z_ready, i * R_HEADS + (head + 1 + len(WINDOWS)))
                            for tap in range(TAPS):
                                w_at = tile + (TAPS - 1 - tap) * NT
                                for m in range(2):
                                    src = z[:, m, PAD - tap:PAD + S - tap]
                                    if tap == 0:
                                        last = v.tensor_scalar(xr[:, m], src, col("conv_w", w_at + m), col("conv_b", tile + m),
                                                               ALU.mult, ALU.add)
                                    else:
                                        last = v.scalar_tensor_tensor(xr[:, m], src, col("conv_w", w_at + m), xr[:, m],
                                                                      ALU.mult, ALU.add)
                                    if tap == TAPS - 1:
                                        last.then_inc(xr_ready, 1)
                                if tap < TAPS - 1:
                                    own.done(last)
                                if tap == 2:
                                    split(U_R + head * R_SEG + 4 + 2, i, n)
                                if tap < TAPS - 1:
                                    own.wait(v)
                        if k == 6:
                            v.wait_ge(gates_ready, nth)
                            step_(v.tensor_tensor(inp[:], inp[:], xr[:], ALU.mult))
                            macs(seg, 3, i, R_HEADS)
                        if k == 7:
                            v.wait_ge(decay_sq, nth)
                            v.scalar_tensor_tensor(tanh_q[:], z[:, :, PAD:], 1.0, tanh_q[:], ALU.add, ALU.mult
                                                   ).then_inc(var_ready, 1)
                        if k == 8:
                            v.wait_ge(root_ready, nth)
                            step_(v.tensor_tensor(inp[:], inp[:], tanh_q[:], ALU.mult))
                            for m in range(2):
                                last = v.tensor_tensor_scan(z[:, m, PAD:], decay[:, m], inp[:, m], 0.0, ALU.mult, ALU.add)
                            step_(last)
                            v.wait_ge(gelu_ready, nth)
                            v.tensor_tensor(gelu[:], z[:, :, PAD:], gelu[:], ALU.mult).then_inc(ya_f, 1)
                            v.wait_ge(ya_hi_ready, nth)
                            ts = bass.ds(v.snap(tile), 2)
                            low(br_lo[:, ts], gelu[:], br_hi[:, ts], ya_lo_ready)
                own.end(R_TURNS)
            modulation(R_BLOCK + HEADS - 1, 4)
            v.wait_ge(mod_ready, R_BLOCK + HEADS)
            step_(v.scalar_tensor_tensor(sm["gain2"][:], mod[:, SC2:SC2 + NT], 1.0, col("g_ffn", 0, NT), ALU.add, ALU.mult))

            def merge_position(k, i):
                split(U_M + k + 2, i, 8)
                if k == 7:
                    v.wait_ge(gate_ready, i + (PAIRS + 1))
                    step_(v.tensor_tensor(gate_a[:], ps[:, 2:4], gate_a[:], ALU.mult))
                    v.wait_ge(pb_back, i * 16 + 16)
                    pair = 2 * i if isinstance(i, int) else v.snap(i * 2)
                    v.tensor_tensor(merged[:, span(pair, 2)], gate_a[:], pb_in[:], ALU.add).then_inc(merged_ready, 1)

            def merge_lo(d):
                v.wait_ge(mg_hi, d + 1)
                low(col_lo[:, 2 * d:2 * d + 2], merged[:, 2 * d:2 * d + 2], col_hi[:, 2 * d:2 * d + 2], mg_lo)

            with v.Fori(0, PAIRS - 1) as i:
                own.loop(i, 1)
                for k in range(8):
                    merge_position(k, i)
                own.end(PAIRS - 1)
            for k in range(8):
                merge_position(k, PAIRS - 1)
                for d in MERGE_AT.get(k, ()):
                    merge_lo(d)

            def add_squares(count):
                v.wait_ge(sq_ready, count)
                if not isinstance(count, int) or count > 1:
                    v.wait_ge(sq_used, count - 1)
                step_(v.tensor_tensor(sq_sum[:], sq_sum[:], sq[:, 0], ALU.add))
                v.tensor_tensor(sq_sum[:], sq_sum[:], sq[:, 1], ALU.add).then_inc(sq_used, 1)

            def add_out(d, b, i=None):
                tile = 2 * d if i is None else i * 4 + 2 * d
                for m in range(2):
                    r = resid[:, 2 * d + m] if i is None else resid[:, bass.ds(v.snap(tile + m), 1)].rearrange("p a s -> p (a s)")
                    last = v.scalar_tensor_tensor(r, ps[:, b + m], cols(mod, tile + (GT1 + m)), r, ALU.mult, ALU.add)
                last.then_inc(x2_ready, 1)

            merge_lo(PAIRS - 2)
            for k in range(8):
                if k == 3:
                    step_(v.memset(sq_sum[:], 0.0))
                split(U_O + k + 2)
                if k == 0:
                    merge_lo(PAIRS - 1)
                if k % 4 == 3:
                    v.wait_ge(resid_in[0], 16)
                    add_out(k // 4, 2 * (k // 4))
                    add_squares(k // 4 + 1)
            for q in range(1, NQ):
                v.wait_ge(resid_in[q], 16)
            with v.Fori(0, 3) as i:
                own.loop(i, 2)
                for half in range(2):
                    for k in range(4):
                        u = U_O + 8 + half * 4 + k
                        if k == 3:
                            v.wait_ge(unit_done, i * 8 + (u + 1))
                            add_out(half + 2, 2 * half, i)
                        split(u + 2, i, 8)
                        if k == 3:
                            add_squares(i * 2 + (half + 3))
                own.end(3)
            v.wait_ge(sum2, 1)
            v.tensor_scalar(row_rstd[:], ps[:, 4, 0:ST], 1.0 / D, EPS, ALU.mult, ALU.add).then_inc(var2, 1)
            v.wait_ge(std2, 1)
            widen_rstd()
            v.wait_ge(rstd_spread, 2)

            def xn2(t):
                if t >= QT:
                    v.wait_ge(h2_lo, t - QT + 1)
                if t == 2:
                    v.tensor_copy(rstd_bc[:], ps[:, 5]).then_inc(rstd_ready, 1)
                    v.wait_ge(rstd_ready, 2)
                v.tensor_tensor(h2f[:, t % QT], resid[:, t], ps[:, 5] if t < 2 else rstd_bc[:], ALU.mult
                                ).then_inc(xn2_ready, 1)

            def h2_low(t):
                v.wait_ge(h2_hi, t + 1)
                low(col_lo[:, t], h2f[:, t % QT], col_hi[:, t], h2_lo)

            def conv_taps(pair, b, nth, g4):
                buf = conv_l if pair % 2 else conv_a
                v.wait_ge(tap_ready, nth)
                for tap in (1, 2):
                    for m in range(2):
                        tile = (2 * (pair // 2) + m + (pair % 2) * (DF // P)) + g4
                        last = v.scalar_tensor_tensor(buf[:, m, tap:], ps[:, b + m, 0:S - tap],
                                                      col("ffn_w1" if tap == 1 else "ffn_w0", tile), buf[:, m, tap:],
                                                      ALU.mult, ALU.add)
                    if tap == 1:
                        step_(last)
                last.then_inc(conv_ready, 1)

            def make_u(pair, nth_conv, nth_silu, nth):
                k = pair // 2
                v.wait_ge(conv_ready, nth_conv)
                v.wait_ge(silu_ready, nth_silu)
                v.tensor_tensor(conv_l[:], silu_a[:, k], conv_l[:], ALU.mult).then_inc(uf_ready, 1)
                v.wait_ge(u_hi_ready, nth)
                low(u_lo[:, 2 * k:2 * k + 2], conv_l[:], u_hi[:, 2 * k:2 * k + 2], u_lo_ready)

            def add_down(d, b=None):
                b = 4 + 2 * (d % 2) if b is None else b
                for m in range(2):
                    t = 2 * d + m
                    last = v.scalar_tensor_tensor(resid[:, t], ps[:, b + m], mod[:, GT2 + t:GT2 + t + 1],
                                                  resid[:, t], ALU.mult, ALU.add)
                last.then_inc(down_added, 1)

            xn2(0)
            for t in range(QT):
                if t + 1 < QT:
                    xn2(t + 1)
                h2_low(t)
            for k in range(16):
                if k + QT < NT:
                    xn2(k + QT)
                    h2_low(k + QT)
                split(U_F + k + 2)
                if k >= 12:
                    pair = k - 12
                    conv_taps(pair, 2 * pair, pair + 1, 0)
                    if pair % 2:
                        make_u(pair, pair + 1, pair // 2 + 1, pair // 2 + 1)
            with v.Fori(0, GROUPS - 1) as i:
                own.loop(i, 4)
                for k in range(F_SEG):
                    split(U_L + k + 2, i, F_SEG)
                    if 4 <= k < 12:
                        add_down(k - 4)
                    if k in (3, 15, 19, 23):
                        pair = (3, 15, 19, 23).index(k)
                        conv_taps(pair, 2 * pair, i * 4 + (5 + pair), i * QT + QT)
                        if pair % 2:
                            make_u(pair, i * 4 + (5 + pair), i * 2 + (3 + pair // 2), i * 2 + (3 + pair // 2))
                own.end(GROUPS - 1)
            step_(v.memset(sq_sum[:], 0.0))
            for d in range(8):
                if U_D + d + 2 < UNITS:
                    split(U_D + d + 2)
                v.wait_ge(unit_done, U_D + d + 1)
                add_down(d, 2 if d == 1 else None)
                add_squares(PAIRS + d + 1)
            v.wait_ge(sum3, 1)
            v.tensor_scalar(row_rstd[:], ps[:, 4, 0:ST], 1.0 / D, EPS, ALU.mult, ALU.add).then_inc(var3, 1)
            v.wait_ge(std3, 1)
            v.reciprocal(row_rstd[:], row_rstd[:]).then_inc(rstd3, 1)
            v.wait_ge(rstd3, 1)
            for s in DVE_ROWS:
                for half, cs in enumerate(OUT_PARTS):
                    last = v.tensor_scalar(rows_out[:, s, cs], rows_out[:, s, cs], row_rstd[:, s:s + 1], None, ALU.mult)
                    if half:
                        v.wait_ge(turned, PAIRS)
                        last = v.tensor_scalar(rows_out[:, s, D - UC:], ps[:, 2, (s % 2) * UC:(s % 2 + 1) * UC],
                                               row_rstd[:, s:s + 1], None, ALU.mult)
                    last.then_inc(rows_dve, 1)


_INS = ['x', 'c', 'ada_w', 'ada_b', 'norm_mix_g', 'w_in', 'b_in', 'conv_w', 'conv_b', 'lru_wa', 'lru_ba', 'lru_wx',
        'lru_bx', 'lru_lambda', 'pool_w', 'pool_b', 'pool_scale', 'proj_a', 'proj_b', 'w_out', 'norm_ffn_g', 'w_up',
        'ffn_conv_w', 'ffn_conv_b', 'w_down', 'final_g']
_OUTS = [((1, 512, 2048), 'float32')]


def kernel(**inputs):
    import numpy as _np
    import concourse.bacc as _bacc
    from concourse import mybir as _mybir
    from concourse.bass_utils import run_bass_kernel_spmd as _run

    nc = _bacc.Bacc("TRN2", target_bir_lowering=False, num_devices=1)
    arrays, args = {}, []
    for name in _INS:
        a = _np.ascontiguousarray(inputs[name])
        arrays[f"in_{name}_dram"] = a
        args.append(nc.dram_tensor(f"in_{name}_dram", a.shape, _mybir.dt.from_np(a.dtype), kind="ExternalInput").ap())
    for i, (shape, dtype) in enumerate(_OUTS):
        dt = _mybir.dt.from_np(_np.dtype(dtype))
        args.append(nc.dram_tensor(f"out_{i}_dram", shape, dt, kind="ExternalOutput").ap())
    trunk_kernel(nc, *args)
    r = _run(nc, [arrays], core_ids=[0])
    got = tuple(r.results[0][f"out_{i}_dram"] for i in range(len(_OUTS)))
    return got[0]
```
